# Optimizing a Trainium2 kernel written in Bass

```python
import math
import jax, jax.numpy as jnp
from jax import lax
import numpy as np

D_MODEL = 1024
BATCH = 1
SEQ = 256
DEPTH = 2

RET_HEADS = 4
RET_DK = 64
RET_DV = 128
RET_CHUNK = 128
DSA_HEADS = 8
DSA_DH = 64
DSA_Q_RANK = 256
DSA_KV_RANK = 128
IDX_HEADS = 8
IDX_DIM = 64
DSA_TOPK_MAX = 256
Q_BLOCK = 128
HGRN_HEADS = 4
HGRN_EXPAND = 128
HGRN_DV = 128
HGRN_CHUNK = 32
F_FLOOR = 1e-6
REL_BUCKETS = 32
REL_MAX_DIST = 128
D_FF = 2816
CONV_WIDTH = 3
EPS = 1e-6
NEG_BIG = -1e30

RET_W = RET_HEADS * RET_DV
DSA_W = DSA_HEADS * DSA_DH
HGRN_KW = HGRN_HEADS * HGRN_EXPAND
HGRN_W = HGRN_HEADS * HGRN_DV
N_BRANCH = 3
IN_WIDTHS = (RET_HEADS * RET_DK, RET_HEADS * RET_DK, RET_W, RET_W,
             DSA_Q_RANK, DSA_KV_RANK, IDX_DIM, IDX_HEADS,
             HGRN_KW, HGRN_KW, HGRN_W, HGRN_W,
             N_BRANCH * D_MODEL)
D_IN = sum(IN_WIDTHS)
DSA_UQ_OUT = DSA_HEADS * DSA_DH + IDX_HEADS * IDX_DIM

kernel_name = "hybrid_ret_dsa_hgrn2_gated"

F32 = jnp.float32

def rms_norm(x, g):
    xf = x.astype(F32)
    y = xf * lax.rsqrt(jnp.mean(xf * xf, axis=-1, keepdims=True) + EPS)
    return (y * g.astype(F32)).astype(x.dtype)

def split_columns(z):
    offsets, acc = [], 0
    for w in IN_WIDTHS[:-1]:
        acc += w
        offsets.append(acc)
    return jnp.split(z, offsets, axis=-1)

def rotary(x, pos):
    half = x.shape[-1] // 2
    freq = 1.0 / (10000.0 ** jnp.linspace(0.0, 1.0, half, dtype=F32))
    ang = pos[:, None] * freq[None, :]
    cos = jnp.cos(ang)[None, :, None, :]
    sin = jnp.sin(ang)[None, :, None, :]
    x1, x2 = x[..., :half], x[..., half:]
    return jnp.concatenate([x1 * cos - x2 * sin, x1 * sin + x2 * cos], axis=-1)

def masked_softmax(logits, mask):
    z = jnp.where(mask, logits, NEG_BIG)
    e = jnp.exp(z - jnp.max(z, axis=-1, keepdims=True))
    e = jnp.where(mask, e, 0.0)
    return e / jnp.sum(e, axis=-1, keepdims=True)

def retention_branch(q, k, v, g):
    B, T, _ = q.shape
    H, dk, dv = RET_HEADS, RET_DK, RET_DV
    pos = jnp.arange(T, dtype=F32)
    q = rotary(q.reshape(B, T, H, dk).astype(F32), pos)
    k = rotary(k.reshape(B, T, H, dk).astype(F32), pos) * dk ** -0.5
    v = v.reshape(B, T, H, dv).astype(F32)
    log_gamma = jnp.log1p(-(2.0 ** (-5.0 - jnp.arange(H, dtype=F32))))
    C = min(RET_CHUNK, T)
    n = T // C
    i = jnp.arange(C, dtype=F32)
    rel = i[:, None] - i[None, :]
    dmask = jnp.where(rel >= 0, jnp.exp(jnp.maximum(rel, 0.0)[None] * log_gamma[:, None, None]), 0.0)
    xi = jnp.exp((i + 1.0)[None, :] * log_gamma[:, None])
    zeta = jnp.exp((C - 1.0 - i)[None, :] * log_gamma[:, None])
    gamma_c = jnp.exp(C * log_gamma)

    def chunks(a):
        return a.reshape(B, n, C, H, a.shape[-1]).transpose(1, 0, 3, 2, 4)

    def step(R, inp):
        qi, ki, vi = inp
        inner = jnp.einsum('bhts,bhse->bhte', jnp.einsum('bhtd,bhsd->bhts', qi, ki) * dmask, vi)
        cross = jnp.einsum('bhtd,bhde->bhte', qi, R) * xi[None, :, :, None]
        R = gamma_c[None, :, None, None] * R + jnp.einsum('bhsd,bhse->bhde', ki * zeta[None, :, :, None], vi)
        return R, inner + cross

    _, o = lax.scan(step, jnp.zeros((B, H, dk, dv), F32), (chunks(q), chunks(k), chunks(v)))
    o = o.transpose(1, 0, 3, 2, 4).reshape(B, T, H, dv)
    mu = jnp.mean(o, axis=-1, keepdims=True)
    var = jnp.mean((o - mu) ** 2, axis=-1, keepdims=True)
    o = ((o - mu) * lax.rsqrt(var + EPS)).reshape(B, T, H * dv)
    return (jax.nn.silu(g.astype(F32)) * o).astype(g.dtype)

def rel_bucket(n):
    max_exact = REL_BUCKETS // 2
    nf = jnp.maximum(n, max_exact).astype(F32)
    large = max_exact + (jnp.log(nf / max_exact) / math.log(REL_MAX_DIST / max_exact)
                         * (REL_BUCKETS - max_exact)).astype(jnp.int32)
    large = jnp.minimum(large, REL_BUCKETS - 1)
    return jnp.where(n < max_exact, n, large)

def dsa_branch(c_q, c_kv, idx_k, idx_w, q_norm, kv_norm, w_uq, w_uk, w_uv, rel_bias):
    B, T, _ = c_q.shape
    H, dh, HI, dI = DSA_HEADS, DSA_DH, IDX_HEADS, IDX_DIM
    c_q = rms_norm(c_q, q_norm)
    c_kv = rms_norm(c_kv, kv_norm)
    qq = c_q @ w_uq
    q = qq[..., :H * dh].reshape(B, T, H, dh)
    q_idx = qq[..., H * dh:].reshape(B, T, HI, dI)
    q_lat = jnp.einsum('bthd,hdc->bthc', q, w_uk) * dh ** -0.5
    w_idx = idx_w * (HI * dI) ** -0.5
    Qb = min(Q_BLOCK, T)
    nb = T // Qb
    K = min(DSA_TOPK_MAX, T // 4)
    key_pos = jnp.arange(T, dtype=jnp.int32)
    starts = jnp.arange(nb, dtype=jnp.int32) * Qb

    def blocks(a):
        return a.reshape((B, nb, Qb) + a.shape[2:]).swapaxes(0, 1)

    def attend_block(inp):
        ql, qi, wi, t0 = inp
        t = t0 + jnp.arange(Qb, dtype=jnp.int32)
        score = jnp.einsum('bqsh,bqh->bqs', jax.nn.relu(jnp.einsum('bqhd,bsd->bqsh', qi, idx_k)), wi)
        score = jnp.where(key_pos[None, None, :] <= t[None, :, None], score.astype(F32), NEG_BIG)
        _, sel = lax.top_k(score, K)
        valid = sel <= t[None, :, None]
        c_sel = jax.vmap(lambda c, s: c[s])(c_kv, sel)
        bias = jnp.take(rel_bias, rel_bucket(jnp.maximum(t[None, :, None] - sel, 0)), axis=0)
        logits = jnp.einsum('bqhc,bqkc->bqhk', ql, c_sel).astype(F32) + jnp.moveaxis(bias, -1, 2).astype(F32)
        probs = masked_softmax(logits, valid[:, :, None, :]).astype(c_sel.dtype)
        o_lat = jnp.einsum('bqhk,bqkc->bqhc', probs, c_sel)
        return jnp.einsum('bqhc,hcd->bqhd', o_lat, w_uv).reshape(B, Qb, H * dh)

    out = lax.map(attend_block, (blocks(q_lat), blocks(q_idx), blocks(w_idx), starts))
    return out.swapaxes(0, 1).reshape(B, T, H * dh)

def hgrn2_branch(q, f_logit, v, g, lb, norm_gain):
    B, T, _ = q.shape
    H, dk, dv = HGRN_HEADS, HGRN_EXPAND, HGRN_DV
    z = f_logit.astype(F32)
    lb = jnp.clip(lb.astype(F32), 0.0, 1.0)
    f = lb + (1.0 - lb) * jax.nn.sigmoid(z)
    log_f = jnp.log(jnp.maximum(f, F_FLOOR))
    k = (1.0 - lb) * jax.nn.sigmoid(-z)
    C = min(HGRN_CHUNK, T)
    n = T // C

    def chunks(a, d):
        return a.astype(F32).reshape(B, n, C, H, d).transpose(1, 0, 3, 2, 4)

    causal = jnp.tril(jnp.ones((C, C), dtype=bool))[None, None, :, :, None]

    def step(S, inp):
        qi, ki, vi, fi = inp
        b = jnp.cumsum(fi, axis=2)
        diff = b[:, :, :, None, :] - b[:, :, None, :, :]
        decay = jnp.where(causal, jnp.exp(jnp.where(causal, diff, 0.0)), 0.0)
        attn = jnp.einsum('bhtc,bhsc,bhtsc->bhts', qi, ki, decay)
        o = jnp.einsum('bhts,bhse->bhte', attn, vi) + jnp.einsum('bhtc,bhce->bhte', qi * jnp.exp(b), S)
        b_last = b[:, :, -1:, :]
        S = jnp.exp(b_last[:, :, 0, :])[..., None] * S + jnp.einsum('bhsc,bhse->bhce', ki * jnp.exp(b_last - b), vi)
        return S, o

    _, o = lax.scan(step, jnp.zeros((B, H, dk, dv), F32),
                    (chunks(q, dk), chunks(k, dk), chunks(v, dv), chunks(log_f, dk)))
    o = o.transpose(1, 0, 3, 2, 4).reshape(B, T, H * dv)
    o = rms_norm(o, norm_gain)
    return (jax.nn.silu(g.astype(F32)) * o).astype(g.dtype)

def causal_depthwise_conv(h, w, b):
    C = h.shape[-1]
    y = lax.conv_general_dilated(h, w[:, None, :], window_strides=(1,), padding=[(CONV_WIDTH - 1, 0)],
                                 dimension_numbers=('NWC', 'WIO', 'NWC'), feature_group_count=C)
    return y + b

def conv_ffn(x, w_up, conv_w, conv_b, w_down):
    h = causal_depthwise_conv(x @ w_up, conv_w, conv_b)
    a, u = jnp.split(h, 2, axis=-1)
    return (jax.nn.gelu(a) * u) @ w_down

def setup_inputs(seed: int = 0) -> dict:
    key = jax.random.key(seed)
    ks = jax.random.split(key, 24)
    L = DEPTH

    def nrm(k, shape, fan_in):
        return jax.random.normal(k, shape, F32) * fan_in ** -0.5

    def gain(k, shape):
        return 1.0 + 0.02 * jax.random.normal(k, shape, F32)

    return {
        "x": jax.random.normal(ks[0], (BATCH, SEQ, D_MODEL), F32),
        "rel_bias": 0.5 * jax.random.normal(ks[1], (REL_BUCKETS, DSA_HEADS), F32),
        "hgrn_lb": jax.random.normal(ks[2], (L, HGRN_KW), F32),
        "ln_mix_pre": gain(ks[3], (L, D_MODEL)),
        "ln_mix_post": gain(ks[4], (L, D_MODEL)),
        "ln_ffn_pre": gain(ks[5], (L, D_MODEL)),
        "ln_ffn_post": gain(ks[6], (L, D_MODEL)),
        "w_in": nrm(ks[7], (L, D_MODEL, D_IN), D_MODEL),
        "dsa_q_norm": gain(ks[8], (L, DSA_Q_RANK)),
        "dsa_kv_norm": gain(ks[9], (L, DSA_KV_RANK)),
        "dsa_w_uq": nrm(ks[10], (L, DSA_Q_RANK, DSA_UQ_OUT), DSA_Q_RANK),
        "dsa_w_uk": nrm(ks[11], (L, DSA_HEADS, DSA_DH, DSA_KV_RANK), DSA_DH),
        "dsa_w_uv": nrm(ks[12], (L, DSA_HEADS, DSA_KV_RANK, DSA_DH), DSA_KV_RANK),
        "hgrn_norm": gain(ks[13], (L, HGRN_W)),
        "w_br_ret": nrm(ks[14], (L, RET_W, D_MODEL), RET_W),
        "w_br_dsa": nrm(ks[15], (L, DSA_W, D_MODEL), DSA_W),
        "w_br_hgrn": nrm(ks[16], (L, HGRN_W, D_MODEL), HGRN_W),
        "w_out": nrm(ks[17], (L, D_MODEL, D_MODEL), D_MODEL),
        "ffn_w_up": nrm(ks[18], (L, D_MODEL, 2 * D_FF), D_MODEL),
        "ffn_conv_w": nrm(ks[19], (L, CONV_WIDTH, 2 * D_FF), CONV_WIDTH),
        "ffn_conv_b": 0.01 * jax.random.normal(ks[20], (L, 2 * D_FF), F32),
        "ffn_w_down": nrm(ks[21], (L, D_FF, D_MODEL), D_FF),
    }

def reference(x, rel_bias, hgrn_lb, ln_mix_pre, ln_mix_post, ln_ffn_pre, ln_ffn_post, w_in,
              dsa_q_norm, dsa_kv_norm, dsa_w_uq, dsa_w_uk, dsa_w_uv, hgrn_norm,
              w_br_ret, w_br_dsa, w_br_hgrn, w_out, ffn_w_up, ffn_conv_w, ffn_conv_b, ffn_w_down):
    B, T, D = x.shape
    lb_soft = jax.nn.softmax(hgrn_lb.astype(F32), axis=0)
    lower_bounds = jnp.cumsum(lb_soft, axis=0) - lb_soft[0:1]
    for l in range(DEPTH):
        h = rms_norm(x, ln_mix_pre[l])
        (rq, rk, rv, rg, cq, ckv, ik, iw, hq, hf, hv, hg, gt) = split_columns(h @ w_in[l])
        y_ret = retention_branch(rq, rk, rv, rg)
        y_dsa = dsa_branch(cq, ckv, ik, iw, dsa_q_norm[l], dsa_kv_norm[l], dsa_w_uq[l], dsa_w_uk[l],
                           dsa_w_uv[l], rel_bias)
        y_hg = hgrn2_branch(hq, hf, hv, hg, lower_bounds[l], hgrn_norm[l])
        gates = jax.nn.sigmoid(gt).reshape(B, T, N_BRANCH, D)
        merged = (gates[:, :, 0] * (y_ret @ w_br_ret[l])
                  + gates[:, :, 1] * (y_dsa @ w_br_dsa[l])
                  + gates[:, :, 2] * (y_hg @ w_br_hgrn[l]))
        x = x + rms_norm(merged @ w_out[l], ln_mix_post[l])
        h = rms_norm(x, ln_ffn_pre[l])
        x = x + rms_norm(conv_ffn(h, ffn_w_up[l], ffn_conv_w[l], ffn_conv_b[l], ffn_w_down[l]), ln_ffn_post[l])
    return x


_drawn_inputs = setup_inputs


def setup_inputs(seed=0):
    import zlib

    import numpy as np

    out = dict(_drawn_inputs(seed))
    spreads = {}
    factors = {'ffn_conv_b': 2.799}
    for name, (base, spread) in spreads.items():
        noise = np.random.default_rng([zlib.crc32(name.encode()), seed]).standard_normal(out[name].shape)
        drawn = base * np.exp(spread * noise) if base else spread * noise
        out[name] = __import__('jax').numpy.asarray(drawn.astype(out[name].dtype))
    for name, factor in factors.items():
        out[name] = (out[name] * factor).astype(out[name].dtype)
    return out
```

```python
from contextlib import ExitStack

import numpy as np

import concourse.bass as bass
from concourse import mybir

ALU = mybir.AluOpType
ACT = mybir.ActivationFunctionType
F32 = mybir.dt.float32
F32R = mybir.dt.float32r
U32 = mybir.dt.uint32
AX_X = mybir.AxisListType.X

P = 128
T = 256
TT = T // P
D = 1024
KD = D // P
HR, DKR = 4, 64
HD, DH, QR, KVR = 8, 64, 256, 128
TOPK = 64
HG = 4
DFF = 2816
NPAIR = DFF // (2 * P)
EPS = 1e-6
FLOOR = 1e-6
NEG = -1e30
TAKEN = -3e38
UNIT = 2048
SLOTS = 3
LEVELS = 7

C_RQ, C_RK, C_RV, C_RG = 0, 256, 512, 1024
C_CQ, C_KV = 1536, 1792
C_HQ, C_HF, C_HV, C_HG, C_GT = 1992, 2504, 3016, 3528, 4040

U_CQ, U_KV, U_HF, U_HQ, U_UQ, U_RQ, U_RK = 0, 1, 2, 4, 6, 7, 8
U_HV, U_RV, U_RG, U_HGATE, U_GT, U_BR, U_WO, U_FF = 9, 11, 13, 15, 17, 29, 35, 39
UNITS = U_FF + 3 * NPAIR
PER_SLOT = UNITS // SLOTS
assert UNITS % SLOTS == 0

Q_PRE, Q_FFN, Q_QN, Q_KVN, Q_HGN, Q_LB, Q_CB, Q_CW = 0, 8, 16, 18, 19, 23, 27, 71
NPRM = Q_CW + 3 * 44
ROWS_A = Q_CW + 44

K_ID, K_ROT, K_ONE, K_COS, K_SIN, K_DM, K_CM, K_LV, K_OH = 0, 128, 256, 384, 640, 896, 1920, 2304, 2752
K_ALL = K_OH + 384


def shape_constants():
    f = np.float32
    k = np.zeros((P, K_ALL), f)
    i = np.arange(P)
    k[:, K_ID:K_ID + P] = np.eye(P)
    for d in range(P):
        if d % 64 < 32:
            k[d + 32, K_ROT + d] = -1.0
        else:
            k[d - 32, K_ROT + d] = 1.0
    k[:, K_ONE:K_ONE + P] = 1.0
    freq = (f(1.0) / np.power(f(10000.0), np.linspace(0.0, 1.0, 32, dtype=f))).astype(f)
    ang = (np.arange(T, dtype=f)[None, :] * freq[i % 32][:, None]).astype(f)
    k[:, K_COS:K_COS + T] = np.cos(ang)
    k[:, K_SIN:K_SIN + T] = np.sin(ang)
    log_gamma = np.log1p(-(2.0 ** (-5.0 - np.arange(HR))))
    rel = np.arange(T)[None, :] - i[:, None]
    for h in range(HR):
        k[:, K_DM + h * T:K_DM + (h + 1) * T] = np.where(rel >= 0, np.exp(np.maximum(rel, 0) * log_gamma[h]), 0) * DKR ** -0.5
    k[:, K_CM:K_CM + P] = np.where(i[None, :] <= i[:, None], 0.0, NEG)
    k[:, K_CM + P:K_CM + 3 * P] = np.where(np.arange(T)[None, :] <= P + i[:, None], 0.0, NEG)
    for v in range(LEVELS):
        m = 1 << v
        for c in range(64):
            b = c // m
            k[2 * b * m:(2 * b + 1) * m, K_LV + 64 * v + c] = 1.0
    n = np.maximum(256 - np.arange(384), 0)
    nf = np.maximum(n, 16).astype(f)
    large = 16 + (np.log(nf / f(16)) / f(np.log(8.0)) * f(16)).astype(np.int32)
    bucket = np.where(n < 16, n, np.minimum(large, 31))
    k[bucket, K_OH + np.arange(384)] = 1.0
    return k


def trunk(nc, consts, x, rel_bias, hgrn_lb, ln_mix_pre, ln_mix_post, ln_ffn_pre, ln_ffn_post, w_in,
          dsa_q_norm, dsa_kv_norm, dsa_w_uq, dsa_w_uk, dsa_w_uv, hgrn_norm,
          w_br_ret, w_br_dsa, w_br_hgrn, w_out, ffn_w_up, ffn_conv_w, ffn_conv_b, ffn_w_down, out):
    DEPTH = w_in.shape[0]
    scratch = nc.dram_tensor("bias_rows", (P, HD, 384), F32, kind="Internal").ap()

    with ExitStack() as ctx:
        arena = ctx.enter_context(nc.sbuf_tensor("arena", [P, 53200], F32))
        base = 16512
        here = [base]

        def at(name, offset, shape, dt=F32):
            return nc.alloc_sbuf_tensor_at(name, shape, dt, offset=offset)

        def keep(name, shape, dt=F32):
            n = 4
            for s in shape[1:]:
                n *= s
            o = here[0]
            here[0] += (n + 31) // 32 * 32
            return at(name, o, shape, dt)

        def room(nbytes):
            o = here[0]
            here[0] += nbytes
            return o

        kc = keep("kc", [P, K_OH])
        raw = [keep(f"raw{i}", [P, UNIT]) for i in range(SLOTS)]
        up = [keep(f"up{i}", [P, UNIT], F32R) for i in range(SLOTS)]
        low = [keep(f"low{i}", [P, UNIT], F32R) for i in range(SLOTS)]
        xr = keep("xr", [P, TT, D])
        h_up = keep("h_up", [P, KD, T], F32R)
        h_low = keep("h_low", [P, KD, T], F32R)
        bias = keep("bias", [P, HD, T])
        prm_all = keep("prm_all", [P, DEPTH, NPRM])
        prm = keep("prm", [P, NPRM])
        lbs = keep("lbs", [P, DEPTH, 4, 4])
        w_uk = keep("w_uk", [P, 4, P])
        w_uv = keep("w_uv", [P, HD, DH])
        r_gate, r_dsa, r_hg, r_ret = room(24 * 1024), room(8 * 1024), room(8 * 1024), room(8 * 1024)
        gates = at("gates", r_gate, [P, 24, T])
        xs = at("xs", r_gate, [P, TT, D])
        junk = at("junk", r_gate + 8192, [P, D])
        hgq = at("hgq", r_gate, [P, HG * T])
        hgk = at("hgk", r_gate + 4096, [P, HG * T])
        hgf = at("hgf", r_gate + 8192, [P, HG * T])
        qk = at("qk", r_gate + 12288, [P, 4, T])
        qkcos = at("qkcos", r_gate + 16384, [P, 4, T])
        qkr = at("qkr", r_gate + 20480, [P, 4, T])
        ydsa_up = at("ydsa_up", r_dsa, [P, 4, T], F32R)
        ydsa_low = at("ydsa_low", r_dsa + 4096, [P, 4, T], F32R)
        zs = at("zs", r_dsa, [P, 3, T])
        ikT = at("ikT", r_dsa + 3072, [P, T])
        cq_up = at("cq_up", r_dsa + 4096, [P, 2, T], F32R)
        cq_low = at("cq_low", r_dsa + 6144, [P, 2, T], F32R)
        silu_h = at("silu_h", r_dsa, [P, TT, 512])
        silu_r = at("silu_r", r_dsa + 4096, [P, TT, 512])
        yhg_up = at("yhg_up", r_hg, [P, 4, T], F32R)
        yhg_low = at("yhg_low", r_hg + 4096, [P, 4, T], F32R)
        sq = at("sq", r_hg, [P, 3, T])
        qiT = at("qiT", r_hg + 4096, [P, 4, T])
        att = at("att", r_hg, [P, 8, P])
        att2 = at("att2", r_hg + 4096, [P, HG, P])
        yret_up = at("yret_up", r_ret, [P, 4, T], F32R)
        yret_low = at("yret_low", r_ret + 4096, [P, 4, T], F32R)
        qT = at("qT", r_ret, [P, 4, T])
        r_tmp = here[0]
        ckvT = at("ckvT", r_tmp, [P, T])
        cqT = at("cqT", r_tmp + 1024, [P, 2, T])
        vlat = at("vlat", r_tmp + 3072, [P, TT, HD * DH])
        probs = at("probs", r_tmp + 7168, [P, 2, 384])
        score = at("score", r_tmp + 10240, [P, 384])
        mbias = at("mbias", r_tmp + 11776, [P, 2, 384])
        probsT = at("probsT", r_tmp + 14848, [P, 2, 384])
        v_h = at("v_h", r_tmp + 17920, [P, TT, 512])
        v_r = at("v_r", r_tmp + 22016, [P, TT, 512])
        yn_r = v_r
        yn_h = v_h
        dec = at("dec", r_tmp + 26112, [P, HR, 384])
        qlat = at("qlat", r_tmp + 26112, [P, HD, T])
        diag = at("diag", r_tmp + 26112, [P, 4, P])
        hgf2 = at("hgf2", r_tmp + 34304, [P, 512])
        small = at("small", r_tmp + 36352, [P, 192])
        mrg = at("mrg", r_tmp + 17920, [P, 4, T])
        mtmp = at("mtmp", r_tmp + 22016, [P, 4, T])
        xtmp = at("xtmp", r_tmp + 17920, [P, TT, D])
        gpost = at("gpost", r_tmp + 26112, [P, D])
        cva = at("cva", r_tmp, [P, 2, T])
        cvu = at("cvu", r_tmp + 2048, [P, 2, T])
        gel = at("gel", r_tmp + 4096, [P, 2, T])
        gf = at("gf", r_tmp + 6144, [P, 2, T])
        g_up = at("g_up", r_tmp + 8192, [P, 2, T], F32R)
        g_low = at("g_low", r_tmp + 10240, [P, 2, T], F32R)
        cvp = at("cvp", r_tmp + 12288, [P, 4, 2, 2])
        rows = at("rows", r_gate, [P, 4, P])
        onehot = at("onehot", r_gate + 2048, [P, 384])
        relb = at("relb", r_gate + 4096, [P, HD])
        brow = at("brow", r_gate + 5120, [P, 384])
        assert r_tmp + 37000 <= base + 53200 * 4, (r_tmp + 37000, base + 53200 * 4)

        ident, rot = kc[:, K_ID:K_ID + P], kc[:, K_ROT:K_ROT + P]
        ones, cos, sin = kc[:, K_ONE:K_ONE + P], kc[:, K_COS:K_COS + T], kc[:, K_SIN:K_SIN + T]
        cmask = kc[:, K_CM:K_CM + 384]
        nhalf, ss, rs = small[:, 0:8], small[:, 8:16], small[:, 16:24]
        cs4, cr4, wi = small[:, 24:28], small[:, 28:32], small[:, 32:48]
        oss, ors, best8 = small[:, 48:52], small[:, 52:56], small[:, 56:72]
        nmax, rsum, rrec = small[:, 72:76], small[:, 76:80], small[:, 80:84]
        bn6 = small[:, 84:132].rearrange("p (a b) -> p a b", b=6)
        bna = small[:, 132:148].rearrange("p (a b) -> p a b", b=2)
        bnr = small[:, 148:156]
        bnr2, lbc = small[:, 160:168], small[:, 168:176]
        hss = small[:, 156:158]
        hrs = small[:, 158:160]

        ps = ctx.enter_context(nc.psum_tensor("ps", [P, 8, 512], F32))

        def wide(b):
            return ps[:, b:b + 2, :].rearrange("p a b -> p (a b)")

        per_layer = {}

        def sig(name, per):
            s = ctx.enter_context(nc.semaphore(name))
            per_layer[s.name] = per
            return s

        def nth(signal, layer, k):
            return layer * per_layer[signal.name] + k

        raw_in = [sig(f"raw_in{i}", 16 * PER_SLOT) for i in range(SLOTS)]
        up_done = sig("up_done", UNITS)
        low_done = [sig(f"low_done{i}", PER_SLOT) for i in range(SLOTS)]
        unit_used = sig("unit_used", UNITS)
        setup_in, setup_ps, setup_cp, bias_out, bias_in, setup_done, setup_v = (
            sig(n, 1) for n in ("setup_in", "setup_ps", "setup_cp", "bias_out", "bias_in", "setup_done", "setup_v"))
        prm_ready = sig("prm_ready", 1)
        small_in = sig("small_in", 32)
        x_sq, n_var, n_rs, xs_ready = sig("x_sq", 4), sig("n_var", 4), sig("n_rs", 4), sig("xs_ready", 4)
        xT_ready, h_up_done, h_low_done = sig("xT_ready", 8), sig("h_up_done", 8), sig("h_low_done", 8)
        o_ready, o_sq, o_var, o_rs, x_new = sig("o_ready", 2), sig("o_sq", 4), sig("o_var", 4), sig("o_rs", 4), sig("x_new", 4)
        gpost_in = sig("gpost_in", 32)
        evac = sig("evac", 14)
        wi_ready, sq_ready, zs_ready, ss_ready, cvar, crs, diag_ready, bc_ready, c_ready = (
            sig(n, 1) for n in ("wi_ready", "sq_ready", "zs_ready", "ss_ready", "cvar", "crs", "diag_ready", "bc_ready", "c_ready"))
        v_ready, vlat_ready, uqi_ready = sig("v_ready", 1), sig("vlat_ready", 1), sig("uqi_ready", 1)
        idx_ready, relu_done, relu_used = sig("idx_ready", HD), sig("relu_done", HD), sig("relu_used", HD)
        slot_seen = sig("slot_seen", UNITS)
        ik_twice = sig("ik_twice", 16)
        chosen = sig("chosen", 1)
        sg_ready, fk_ready = sig("sg_ready", 1), sig("fk_ready", 1)
        lvl_ready, lvl_next, lvl_used = sig("lvl_ready", 9), sig("lvl_next", 8), sig("lvl_used", 9)
        rot_ready, qkr_ready, dot_ready, dec_ready = sig("rot_ready", 1), sig("qkr_ready", 1), sig("dot_ready", HR), sig("dec_ready", HR)
        oret_ready, bn_var, bn_rs, ynr_ready = sig("oret_ready", 1), sig("bn_var", 1), sig("bn_rs", 1), sig("ynr_ready", 1)
        ohg_ready, ohg_sq, ohg_var, ohg_rs, ynh_ready = (sig(n, 1) for n in ("ohg_ready", "ohg_sq", "ohg_var", "ohg_rs", "ynh_ready"))
        sgr_ready, silur_ready, sgh_ready, siluh_ready = (sig(n, 1) for n in ("sgr_ready", "silur_ready", "sgh_ready", "siluh_ready"))
        yretT, yret_upd, yret_done, yhgT, yhg_upd, yhg_done, ydsa_upd, ydsa_done = (
            sig(n, 1) for n in ("yretT", "yret_upd", "yret_done", "yhgT", "yhg_upd", "yhg_done", "ydsa_upd", "ydsa_done"))
        qlat_ps, qlat_ready = sig("qlat_ps", 2), sig("qlat_ready", 2)
        mb_ready, lg_ready, lg_seen, nmax_ready, exp_done, prob_ready, pT_ps, pT_ready, pv_done = (
            sig(n, HD) for n in ("mb_ready", "lg_ready", "lg_seen", "nmax_ready", "exp_done", "prob_ready", "pT_ps", "pT_ready", "pv_done"))
        br_used, mrg_ready, mrg_up, mrg_done = sig("br_used", 6), sig("mrg_ready", 2), sig("mrg_up", 2), sig("mrg_done", 2)
        cvp_ready, cva_base, cvu_base, cva_done, cvu_done, gel_done, gf_done, gup_done, glow_done = (
            sig(n, NPAIR) for n in ("cvp_ready", "cva_base", "cvu_base", "cva_done", "cvu_done", "gel_done", "gf_done", "gup_done", "glow_done"))
        x_in, y_out = sig("x_in", 16), sig("y_out", 16)

        pool_low = [True, True, False]
        pool_low_ffn = [True, False, False]

        def load_unit(sp, l, u, src, step=0):
            s = u % SLOTS
            sp.wait_ge(low_done[s], l * PER_SLOT + u // SLOTS + step + 1)
            sp.sem_inc(slot_seen, 1)
            sp.dma_start(raw[s][:, :].rearrange("p (a b) -> p a b", a=src.shape[1]), src).then_inc(raw_in[s], 16)

        def split_up(act, l, u, step=0):
            s = u % SLOTS
            act.wait_ge(raw_in[s], 16 * (l * PER_SLOT + u // SLOTS + step + 1))
            act.wait_ge(unit_used, l * UNITS + u + SLOTS * step + 1)
            nc.scalar.activation(up[s][:, :], raw[s][:, :], ACT.Copy).then_inc(up_done, 1)

        def split_low(eng, l, u, step=0):
            s = u % SLOTS
            eng.wait_ge(up_done, l * UNITS + u + SLOTS * step + 1)
            eng.tensor_tensor(low[s][:, :], raw[s][:, :], up[s][:, :].bitcast(F32), ALU.subtract).then_inc(low_done[s], 1)

        def fill(l, u, step=0):
            return l * PER_SLOT + u // SLOTS + step + 2

        def used(l, k, step=0):
            return l * UNITS + k + SLOTS * step + SLOTS

        block = ctx.enter_context(nc.Block())

        @block.sync
        def _(sp):
            sp.dma_start(kc[:, :], consts[:, 0:K_OH]).then_inc(setup_in, 16)
            sp.dma_start(onehot[:, :], consts[:, K_OH:K_ALL]).then_inc(setup_in, 16)
            sp.dma_start(relb[0:32, :], rel_bias).then_inc(setup_in, 16)
            sp.dma_start(xr[:, :, :], x[0].rearrange("(t p) d -> p t d", p=P)).then_inc(x_in, 16)
            for l in range(DEPTH):
                r = 0
                for src in (ln_mix_pre, ln_ffn_pre, dsa_q_norm, dsa_kv_norm, hgrn_norm, hgrn_lb, ffn_conv_b):
                    v = src[l].rearrange("(k p) -> k p", p=P)
                    sp.dma_start(rows[r:r + v.shape[0], 2 * l, :], v).then_inc(setup_in, 16)
                    r += v.shape[0]
                cw = ffn_conv_w[l].rearrange("w (k p) -> (w k) p", p=P)
                sp.dma_start(rows[Q_CW:ROWS_A, 2 * l, :], cw[0:44]).then_inc(setup_in, 16)
                sp.dma_start(rows[0:88, 2 * l + 1, :], cw[44:132]).then_inc(setup_in, 16)
            sp.wait_ge(setup_cp, 1)
            sp.dma_start(scratch.rearrange("t h c -> h t c"), brow[0:HD, None, :].broadcast_to([HD, P, 384])).then_inc(bias_out, 16)
            sp.wait_ge(bias_out, 16)
            skew = bass.AP(scratch.tensor, P, [[HD * 384 - 1, P], [384, HD], [1, T]])
            sp.dma_start(bias[:, :, :], skew).then_inc(bias_in, 16)

            win = w_in.rearrange("l (k p) n -> l p k n", p=P)
            uqv = dsa_w_uq.rearrange("l (k p) n -> l p k n", p=P)
            wov = w_out.rearrange("l (k p) n -> l p k n", p=P)
            brv = [w.rearrange("l (k p) n -> l p k n", p=P) for w in (w_br_ret, w_br_hgrn, w_br_dsa)]
            ukv = dsa_w_uk.rearrange("l (a b) d c -> l (b d) a c", b=2)
            uvv = dsa_w_uv.rearrange("l h c d -> l c h d")
            upv = ffn_w_up.rearrange("l (k p) (g j n) -> l g j p k n", p=P, g=2, n=2 * P)
            dnv = ffn_w_down.rearrange("l (j k p) n -> l j p k n", p=P, k=2)
            with sp.Fori(0, DEPTH) as l:
                W = win[l]
                for u, c in ((U_CQ, C_CQ), (U_KV, C_KV), (U_HF, C_HF), (U_HF + 1, C_HF + 256), (U_HQ, C_HQ), (U_HQ + 1, C_HQ + 256)):
                    load_unit(sp, l, u, W[:, :, c:c + 256])
                    if u == U_HF:
                        sp.dma_start(w_uk[:, :, :], ukv[l]).then_inc(small_in, 16)
                        sp.dma_start(w_uv[:, :, :], uvv[l]).then_inc(small_in, 16)
                load_unit(sp, l, U_UQ, uqv[l])
                load_unit(sp, l, U_RQ, W[:, :, C_RQ:C_RQ + 256])
                load_unit(sp, l, U_RK, W[:, :, C_RK:C_RK + 256])
                for u, c in ((U_HV, C_HV), (U_RV, C_RV), (U_RG, C_RG), (U_HGATE, C_HG)):
                    for half in range(2):
                        load_unit(sp, l, u + half, W[:, 4 * half:4 * half + 4, c:c + 512])
                for g in range(12):
                    load_unit(sp, l, U_GT + g, W[:, :, C_GT + 256 * g:C_GT + 256 * (g + 1)])
                for nb in range(2):
                    for b in range(3):
                        load_unit(sp, l, U_BR + 3 * nb + b, brv[b][l][:, :, 512 * nb:512 * nb + 512])
                for i in range(4):
                    load_unit(sp, l, U_WO + i, wov[l][:, 2 * i:2 * i + 2, :])
                up_l, dn_l = upv[l], dnv[l]
                load_unit(sp, l, U_FF, up_l[0, 0])
                load_unit(sp, l, U_FF + 1, up_l[1, 0])
                load_unit(sp, l, U_FF + 2, up_l[0, 1])
                load_unit(sp, l, U_FF + 3, up_l[1, 1])
                load_unit(sp, l, U_FF + 4, dn_l[0])
                with sp.Fori(0, NPAIR - 2) as j:
                    load_unit(sp, l, U_FF + 5, up_l[0, j + 2], step=j)
                    load_unit(sp, l, U_FF + 6, up_l[1, j + 2], step=j)
                    load_unit(sp, l, U_FF + 7, dn_l[j + 1], step=j)
                load_unit(sp, l, UNITS - 1, dn_l[NPAIR - 1])
            sp.wait_ge(x_new, 4 * DEPTH)
            sp.dma_start(out[0].rearrange("(t p) d -> p t d", p=P), xr[:, :, :]).then_inc(y_out, 16)
            sp.wait_ge(y_out, 16)

        @block.tensor
        def _(pe):
            mm = nc.tensor.matmul

            def three(o, a_up, a_low, b_up, b_low, first, last):
                mm(o, a_up, b_up, start=first, stop=False)
                mm(o, a_up, b_low, start=False, stop=False)
                return mm(o, a_low, b_up, start=False, stop=last)

            def columns_out(s, w, c, n_k, o, a_up, a_low, wait_k=None):
                for k in range(n_k):
                    if wait_k:
                        wait_k(k)
                    wu = up[s][:, :].rearrange("p (k n) -> p k n", n=w)[:, k, c:c + P]
                    wl = low[s][:, :].rearrange("p (k n) -> p k n", n=w)[:, k, c:c + P]
                    i = three(o, wu, wl, a_up[:, k, :], a_low[:, k, :], k == 0, k == n_k - 1)
                return i

            def tokens_out(s, w, ks, k0, o_of, a_up, a_low, first, last):
                for k in range(ks):
                    for t in range(TT):
                        for c in range(w // 512):
                            wu = up[s][:, :].rearrange("p (k n) -> p k n", n=w)[:, k, 512 * c:512 * c + 512]
                            wl = low[s][:, :].rearrange("p (k n) -> p k n", n=w)[:, k, 512 * c:512 * c + 512]
                            au = a_up[:, k0 + k, t * P:(t + 1) * P]
                            al = a_low[:, k0 + k, t * P:(t + 1) * P]
                            o = o_of(t, c)
                            mm(o, au, wu, start=first and k == 0, stop=False)
                            mm(o, au, wl, start=False, stop=False)
                            i = mm(o, al, wu, start=False, stop=last and k == ks - 1)
                return i

            def transposed_x(l, stage):
                for k in range(KD):
                    for t in range(TT):
                        if k == 0:
                            pe.wait_ge(xs_ready, nth(xs_ready, l, 2 * stage + t + 1))
                        i = nc.tensor.transpose(ps[:, 4 + k // 2, (k % 2) * T + t * P:(k % 2) * T + (t + 1) * P],
                                                xs[:, t, k * P:(k + 1) * P], ident)
                    if k % 2:
                        i.then_inc(xT_ready, 1)

            pe.wait_ge(setup_in, 16 * (3 + 9 * DEPTH))
            for i in range(2 * DEPTH):
                n = ROWS_A if i % 2 == 0 else 88
                nc.tensor.transpose(ps[:, 4, i * P:i * P + n], rows[0:n, i, :], kc[0:n, K_ID:K_ID + n])
            mm(ps[0:HD, 5, 0:384], relb[0:32, :], onehot[0:32, :], start=True, stop=True).then_inc(setup_ps, 1)

            with pe.Fori(0, DEPTH) as l:
                transposed_x(l, 0)

                def x_part(k):
                    if k % 2 == 0:
                        pe.wait_ge(h_low_done, nth(h_low_done, l, k // 2 + 1))

                pe.wait_ge(low_done[U_CQ % SLOTS], fill(l, U_CQ))
                columns_out(0, 256, 0, KD, ps[:, 0, 0:T], h_up, h_low, x_part)
                columns_out(0, 256, P, KD, ps[:, 0, T:2 * T], h_up, h_low).then_inc(unit_used, 1)
                pe.wait_ge(low_done[U_KV % SLOTS], fill(l, U_KV))
                columns_out(1, 256, 0, KD, ps[:, 1, 0:T], h_up, h_low)
                columns_out(1, 256, P, KD, ps[:, 1, T:2 * T], h_up, h_low)
                pe.wait_ge(h_low_done, nth(h_low_done, l, 4))
                for t in range(TT):
                    for k in range(KD):
                        wu = up[1][:, :].rearrange("p (k n) -> p k n", n=256)[:, k, 192:200]
                        wl = low[1][:, :].rearrange("p (k n) -> p k n", n=256)[:, k, 192:200]
                        o = ps[:, 7, 8 * t:8 * t + 8]
                        mm(o, h_up[:, k, t * P:(t + 1) * P], wu, start=k == 0, stop=False)
                        mm(o, h_up[:, k, t * P:(t + 1) * P], wl, start=False, stop=False)
                        i = mm(o, h_low[:, k, t * P:(t + 1) * P], wu, start=False, stop=k == KD - 1)
                i.then_inc(unit_used, 1)

                def transposed_unit(u, b):
                    pe.wait_ge(low_done[u % SLOTS], fill(l, u))
                    columns_out(u % SLOTS, 256, 0, KD, ps[:, b, 0:T], h_up, h_low)
                    columns_out(u % SLOTS, 256, P, KD, ps[:, b, T:2 * T], h_up, h_low).then_inc(unit_used, 1)

                def token_units(u, b, half):
                    pe.wait_ge(low_done[(u + half) % SLOTS], fill(l, u + half))
                    tokens_out((u + half) % SLOTS, 512, 4, 4 * half, lambda t, c: ps[:, b + t, :], h_up, h_low,
                               half == 0, half == 1).then_inc(unit_used, 1)

                def sums_of_squares():
                    pe.wait_ge(sq_ready, nth(sq_ready, l, 1))
                    pe.wait_ge(wi_ready, nth(wi_ready, l, 1))
                    for t in range(TT):
                        c = slice(t * P, (t + 1) * P)
                        mm(ps[:, 7, 32 + t:33 + t], sq[:, 0, c], ones[:, 0:1], start=True, stop=False)
                        mm(ps[:, 7, 32 + t:33 + t], sq[:, 1, c], ones[:, 0:1], start=False, stop=True)
                    for t in range(TT):
                        i = mm(ps[:, 7, 34 + t:35 + t], sq[:, 2, t * P:(t + 1) * P], ones[:, 0:1], start=True, stop=True)
                    i.then_inc(ss_ready, 1)

                def spread_rstd():
                    pe.wait_ge(diag_ready, nth(diag_ready, l, 1))
                    mm(ps[:, 6, :], ones, diag[:, :, :].rearrange("p a b -> p (a b)"), start=True, stop=True).then_inc(bc_ready, 1)

                def latent_values():
                    pe.wait_ge(c_ready, nth(c_ready, l, 1))
                    pe.wait_ge(small_in, nth(small_in, l, 32))
                    for t in range(TT):
                        i = mm(ps[:, 4 + t, :], ckvT[:, t * P:(t + 1) * P], w_uv[:, :, :].rearrange("p h d -> p (h d)"),
                               start=True, stop=True)
                    i.then_inc(v_ready, 1)

                def index_scores(h):
                    b, r = 64 * (h % 2), h // 2
                    if h < 2:
                        pe.wait_ge(vlat_ready, nth(vlat_ready, l, 1))
                        pe.wait_ge(ik_twice, nth(ik_twice, l, 16))
                    if h >= 4:
                        pe.wait_ge(relu_done, nth(relu_done, l, h - 3))
                    o = ps[:, 4 + h % 4, :]
                    mm(o[:, 0:P], qiT[b:b + 64, r, 0:P], ikT[b:b + 64, 0:P], start=True, stop=True)
                    mm(o[:, P:3 * P], qiT[b:b + 64, r, P:T], ikT[b:b + 64, :], start=True, stop=True).then_inc(idx_ready, 1)

                def rotate():
                    pe.wait_ge(evac, nth(evac, l, 6))
                    pe.wait_ge(relu_done, nth(relu_done, l, HD))
                    for i4 in range(4):
                        i = mm(ps[:, 4 + i4 // 2, (i4 % 2) * T:(i4 % 2 + 1) * T], rot, qk[:, i4, :], start=True, stop=True)
                    i.then_inc(rot_ready, 1)

                def retention_dots(h):
                    b, r = 64 * (h % 2), h // 2
                    if h == 0:
                        pe.wait_ge(qkr_ready, nth(qkr_ready, l, 1))
                    if h >= 2:
                        pe.wait_ge(dec_ready, nth(dec_ready, l, h - 1))
                    o = ps[:, 4 + h % 2, :]
                    mm(o[:, 0:T], qkr[b:b + 64, 2 + r, 0:P], qkr[b:b + 64, r, :], start=True, stop=True)
                    mm(o[:, T:T + P], qkr[b:b + 64, 2 + r, P:T], qkr[b:b + 64, r, P:T], start=True, stop=True).then_inc(dot_ready, 1)

                def weighted_values(b, first, cross, second, v):
                    for h in range(4):
                        c = slice(h * P, (h + 1) * P)
                        mm(ps[:, b, c], first(h), v[:, 0, c], start=True, stop=True)
                        mm(ps[:, b + 1, c], cross(h), v[:, 0, c], start=True, stop=False)
                        i = mm(ps[:, b + 1, c], second(h), v[:, 1, c], start=False, stop=True)
                    return i

                def retention_out():
                    pe.wait_ge(dec_ready, nth(dec_ready, l, HR))
                    pe.wait_ge(evac, nth(evac, l, 8))
                    weighted_values(4, lambda h: dec[:, h, 0:P], lambda h: dec[:, h, P:T], lambda h: dec[:, h, T:T + P], v_r) \
                        .then_inc(oret_ready, 1)

                def hgrn_level(v):
                    if v == -1:
                        pe.wait_ge(fk_ready, nth(fk_ready, l, 1))
                        pe.wait_ge(evac, nth(evac, l, 3))
                        pe.wait_ge(relu_done, nth(relu_done, l, HD))
                        for a in range(8):
                            c = slice((a % 4) * T + (a // 4) * P, (a % 4) * T + (a // 4) * P + P)
                            i = mm(ps[:, 6 + a // 4, (a % 4) * P:(a % 4 + 1) * P], hgk[:, c], hgq[:, c], start=True, stop=True)
                    else:
                        pe.wait_ge(lvl_next, nth(lvl_next, l, v + 1))
                        if v == 0:
                            pe.wait_ge(lvl_used, nth(lvl_used, l, 1))
                        elif v >= 2:
                            pe.wait_ge(lvl_used, nth(lvl_used, l, v))
                        m = 1 << v
                        b = 6 + v % 2
                        if v < LEVELS:
                            for a in range(8):
                                c = slice((a % 4) * T + (a // 4) * P, (a % 4) * T + (a // 4) * P + P)
                                later = hgq[:, c].rearrange("p (b two m) -> p b two m", two=2, m=m)[:, :, 1, :]
                                i = mm(ps[:, b, a * 64:(a + 1) * 64], hgk[:, c], later, start=True, stop=True)
                        else:
                            for h in range(HG):
                                i = mm(ps[:, b, h * P:(h + 1) * P], hgk[:, h * T:h * T + P], hgq[:, h * T + P:(h + 1) * T], start=True, stop=True)
                    i.then_inc(lvl_ready, 1)

                def hgrn_out():
                    pe.wait_ge(lvl_used, nth(lvl_used, l, 9))
                    pe.wait_ge(evac, nth(evac, l, 7))
                    weighted_values(6, lambda h: att[:, h, :], lambda h: att2[:, h, :], lambda h: att[:, 4 + h, :], v_h) \
                        .then_inc(ohg_ready, 1)

                def transposed_y(b, y, ready, done):
                    pe.wait_ge(ready, nth(ready, l, 1))
                    if b == 4:
                        pe.wait_ge(qlat_ready, nth(qlat_ready, l, 2))
                    for k in range(4):
                        for t in range(TT):
                            i = nc.tensor.transpose(ps[:, b + k // 2, (k % 2) * T + t * P:(k % 2) * T + (t + 1) * P],
                                                    y[:, t, k * P:(k + 1) * P], ident)
                    i.then_inc(done, 1)

                def latent_queries(r):
                    pe.wait_ge(ynr_ready, nth(ynr_ready, l, 1))
                    if r:
                        pe.wait_ge(qlat_ready, nth(qlat_ready, l, 1))
                    for h in range(4 * r, 4 * r + 4):
                        b = 64 * (h % 2)
                        i = mm(ps[:, 4 + h % 2, (h // 2 % 2) * T:(h // 2 % 2 + 1) * T], w_uk[b:b + 64, h // 2, :], qT[b:b + 64, h // 2, :],
                               start=True, stop=True)
                    i.then_inc(qlat_ps, 1)

                def attention_step(h):
                    if h < HD:
                        if h == 0:
                            pe.wait_ge(qlat_ready, nth(qlat_ready, l, 2))
                            pe.wait_ge(yret_done, nth(yret_done, l, 1))
                        if h >= 2:
                            pe.wait_ge(pT_ready, nth(pT_ready, l, h - 1))
                        o = ps[:, 4 + h % 2, :]
                        mm(o[:, 0:P], qlat[:, h, 0:P], ckvT[:, 0:P], start=True, stop=True)
                        mm(o[:, P:3 * P], qlat[:, h, P:T], ckvT[:, :], start=True, stop=True).then_inc(lg_ready, 1)
                    if 1 <= h <= HD:
                        g = h - 1
                        pe.wait_ge(prob_ready, nth(prob_ready, l, g + 1))
                        for c in range(3):
                            i = nc.tensor.transpose(ps[:, 4 + g % 2, c * P:(c + 1) * P], probs[:, g % 2, c * P:(c + 1) * P], ident)
                        i.then_inc(pT_ps, 1)
                    if h >= 2:
                        g = h - 2
                        pe.wait_ge(pT_ready, nth(pT_ready, l, g + 1))
                        if g == 0:
                            pe.wait_ge(yhg_done, nth(yhg_done, l, 1))
                        b, r = 64 * (g % 2), g // 2
                        o = ps[b:b + 64, 6 + r // 2, (r % 2) * T:(r % 2 + 1) * T]
                        mm(o, vlat[:, 0, g * DH:(g + 1) * DH], probsT[:, g % 2, 0:T], start=True, stop=False)
                        mm(o[:, P:T], vlat[:, 1, g * DH:(g + 1) * DH], probsT[:, g % 2, T:T + P], start=False, stop=True) \
                            .then_inc(pv_done, 1)

                transposed_unit(U_HF, 2)
                sums_of_squares()
                transposed_unit(U_HF + 1, 3)
                spread_rstd()
                pe.wait_ge(evac, nth(evac, l, 1))
                transposed_unit(U_HQ, 0)
                transposed_unit(U_HQ + 1, 1)
                latent_values()
                pe.wait_ge(low_done[U_UQ % SLOTS], fill(l, U_UQ))
                pe.wait_ge(evac, nth(evac, l, 2))
                for i in range(4):
                    o = columns_out(0, 1024, 512 + i * P, 2, ps[:, 2 + i // 2, (i % 2) * T:(i % 2 + 1) * T], cq_up, cq_low)
                o.then_inc(uqi_ready, 1)
                pe.wait_ge(evac, nth(evac, l, 3))
                for i in range(4):
                    o = columns_out(0, 1024, i * P, 2, ps[:, i // 2, (i % 2) * T:(i % 2 + 1) * T], cq_up, cq_low)
                o.then_inc(unit_used, 1)
                pe.wait_ge(evac, nth(evac, l, 4))
                transposed_unit(U_RQ, 2)
                for h in range(4):
                    index_scores(h)
                transposed_unit(U_RK, 3)
                for h in range(4, HD):
                    index_scores(h)
                pe.wait_ge(evac, nth(evac, l, 5))
                token_units(U_HV, 0, 0)
                hgrn_level(-1)
                rotate()
                token_units(U_HV, 0, 1)
                hgrn_level(0)
                pe.wait_ge(evac, nth(evac, l, 6))
                token_units(U_RV, 2, 0)
                hgrn_level(1)
                retention_dots(0)
                retention_dots(1)
                token_units(U_RV, 2, 1)
                hgrn_level(2)
                retention_dots(2)
                retention_dots(3)
                pe.wait_ge(evac, nth(evac, l, 7))
                token_units(U_RG, 0, 0)
                hgrn_level(3)
                retention_out()
                token_units(U_RG, 0, 1)
                hgrn_level(4)
                pe.wait_ge(evac, nth(evac, l, 8))
                token_units(U_HGATE, 2, 0)
                hgrn_level(5)
                token_units(U_HGATE, 2, 1)
                hgrn_level(6)
                for g in range(12):
                    u, b = U_GT + g, [0, 1, 2, 3][g % 4]
                    if g == 0:
                        pe.wait_ge(silur_ready, nth(silur_ready, l, 1))
                    elif g == 2:
                        pe.wait_ge(siluh_ready, nth(siluh_ready, l, 1))
                    elif g % 2 == 0:
                        pe.wait_ge(evac, nth(evac, l, 8 + g // 2 - 1))
                    transposed_unit(u, b)
                    if g == 0:
                        hgrn_level(7)
                        latent_queries(0)
                    if g == 1:
                        hgrn_out()
                        latent_queries(1)
                    if g == 2:
                        transposed_y(4, yn_r, ynr_ready, yretT)
                    if g == 3:
                        transposed_y(6, yn_h, ynh_ready, yhgT)
                    if g >= 3:
                        attention_step(g - 3)
                for nb in range(2):
                    for b in range(3):
                        j = 3 * nb + b
                        u = U_BR + j
                        pe.wait_ge(low_done[u % SLOTS], fill(l, u))
                        if j < 2:
                            pe.wait_ge(evac, nth(evac, l, 13 + j))
                        else:
                            pe.wait_ge(br_used, nth(br_used, l, j - 1))
                        if b == 2 and nb == 0:
                            pe.wait_ge(ydsa_done, nth(ydsa_done, l, 1))
                        yu, yl = ((yret_up, yret_low), (yhg_up, yhg_low), (ydsa_up, ydsa_low))[b]
                        for i in range(4):
                            o = columns_out(u % SLOTS, 512, i * P, 4, ps[:, 2 * (j % 2) + i // 2, (i % 2) * T:(i % 2 + 1) * T], yu, yl)
                        o.then_inc(unit_used, 1)
                        if j == 0:
                            attention_step(HD + 1)
                for i in range(4):
                    pe.wait_ge(low_done[(U_WO + i) % SLOTS], fill(l, U_WO + i))
                    if i == 0:
                        pe.wait_ge(br_used, nth(br_used, l, 6))
                    if i % 2 == 0:
                        pe.wait_ge(mrg_done, nth(mrg_done, l, i // 2 + 1))
                    tokens_out((U_WO + i) % SLOTS, 1024, 2, 2 * i, lambda t, c: ps[:, 2 * t + c, :], h_up, h_low, i == 0, i == 3) \
                        .then_inc(unit_used, 1)

                transposed_x(l, 1)

                def ffn_up(u, b, step, wait_x=None):
                    pe.wait_ge(low_done[u % SLOTS], fill(l, u, step))
                    columns_out(u % SLOTS, 256, 0, KD, ps[:, b, 0:T], h_up, h_low, wait_x)
                    columns_out(u % SLOTS, 256, P, KD, ps[:, b, T:2 * T], h_up, h_low).then_inc(unit_used, 1)

                def ffn_down(u, j, step, first, last):
                    pe.wait_ge(low_done[u % SLOTS], fill(l, u, step))
                    pe.wait_ge(glow_done, nth(glow_done, l, j + 1))
                    tokens_out(u % SLOTS, 1024, 2, 0, lambda t, c: ps[:, 2 * t + c, :], g_up, g_low, first, last) \
                        .then_inc(unit_used, 1)

                def ffn_x(k):
                    if k % 2 == 0:
                        pe.wait_ge(h_low_done, nth(h_low_done, l, 4 + k // 2 + 1))

                pe.wait_ge(h_low_done, nth(h_low_done, l, 5))
                ffn_up(U_FF, 4, 0, ffn_x)
                ffn_up(U_FF + 1, 5, 0)
                pe.wait_ge(cva_done, nth(cva_done, l, 1))
                ffn_up(U_FF + 2, 4, 0)
                pe.wait_ge(cvu_done, nth(cvu_done, l, 1))
                ffn_up(U_FF + 3, 5, 0)
                ffn_down(U_FF + 4, 0, 0, True, False)
                with pe.Fori(0, NPAIR - 2) as j:
                    pe.wait_ge(cva_done, nth(cva_done, l, j + 2))
                    ffn_up(U_FF + 5, 4, j)
                    pe.wait_ge(cvu_done, nth(cvu_done, l, j + 2))
                    ffn_up(U_FF + 6, 5, j)
                    ffn_down(U_FF + 7, j + 1, j, False, False)
                ffn_down(UNITS - 1, NPAIR - 1, 0, False, True)

        @block.scalar
        def _(act):
            f = nc.scalar.activation
            act.wait_ge(setup_ps, 1)
            f(brow[0:HD, :], ps[0:HD, 5, 0:384], ACT.Copy).then_inc(setup_cp, 1)
            for i in range(2 * DEPTH):
                n, c = (ROWS_A, 0) if i % 2 == 0 else (88, ROWS_A)
                o = f(prm_all[:, i // 2, c:c + n], ps[:, 4, i * P:i * P + n], ACT.Copy)
            o.then_inc(setup_v, 1)
            act.wait_ge(setup_done, 1)
            for i in range(DEPTH):
                o = f(lbs[:, i, 2, :], lbs[:, i, 3, :], ACT.Exp)
            o.then_inc(setup_v, 1)
            act.wait_ge(x_in, 16)

            with act.Fori(0, DEPTH) as l:
                def x_stage(stage, g0):
                    for t in range(TT):
                        if stage:
                            act.wait_ge(x_new, nth(x_new, l, t + 1))
                        f(junk[:, :], xr[:, t, :], ACT.Square, accum_out=ss[:, t:t + 1]).then_inc(x_sq, 1)
                        act.drain()
                    for k in range(KD):
                        if k % 2 == 0:
                            act.wait_ge(xT_ready, nth(xT_ready, l, 4 * stage + k // 2 + 1))
                        o = f(h_up[:, k, :], ps[:, 4 + k // 2, (k % 2) * T:(k % 2 + 1) * T], ACT.Copy, scale=prm[:, g0 + k:g0 + k + 1])
                        if k % 2:
                            o.then_inc(h_up_done, 1)

                def o_stage(stage):
                    for t in range(TT):
                        f(junk[:, :], wide(2 * t), ACT.Square, accum_out=oss[:, t:t + 1]).then_inc(o_sq, 1)
                        act.drain()

                split_up(act, l, 0)
                split_up(act, l, 1)
                act.wait_ge(prm_ready, nth(prm_ready, l, 1))
                x_stage(0, Q_PRE)
                split_up(act, l, 2)
                act.wait_ge(unit_used, used(l, 1))
                f(sq[:, 0:2, :].rearrange("p a b -> p (a b)"), ps[:, 0, :], ACT.Square)
                for i in range(2):
                    f(zs[:, i, :], ps[:, 0, i * T:(i + 1) * T], ACT.Copy, scale=prm[:, Q_QN + i:Q_QN + i + 1])
                split_up(act, l, 3)
                act.wait_ge(unit_used, used(l, 2))
                f(sq[:, 2, :], ps[:, 1, 0:T], ACT.Square).then_inc(sq_ready, 1)
                f(zs[:, 2, :], ps[:, 1, 0:T], ACT.Copy, scale=prm[:, Q_KVN:Q_KVN + 1]).then_inc(zs_ready, 1)
                f(ikT[0:64, :], ps[0:64, 1, T:2 * T], ACT.Copy).then_inc(evac, 1)
                act.wait_ge(evac, nth(evac, l, 1))
                act.dma_start(ikT[64:128, :], ikT[0:64, :]).then_inc(ik_twice, 16)
                split_up(act, l, 4)
                split_up(act, l, 5)
                act.wait_ge(unit_used, used(l, 4))
                f(hgf[:, :], wide(2), ACT.Sigmoid)
                f(hgk[:, :], wide(2), ACT.Sigmoid, scale=-1.0).then_inc(evac, 1)
                split_up(act, l, 6)
                split_up(act, l, 7)
                act.wait_ge(unit_used, used(l, 6))
                f(hgq[:, :], wide(0), ACT.Copy).then_inc(evac, 1)
                act.wait_ge(v_ready, nth(v_ready, l, 1))
                f(vlat[:, :, :].rearrange("p a b -> p (a b)"), wide(4), ACT.Copy).then_inc(vlat_ready, 1)
                split_up(act, l, 8)
                act.wait_ge(uqi_ready, nth(uqi_ready, l, 1))
                f(qiT[:, :, :].rearrange("p a b -> p (a b)"), wide(2), ACT.Copy).then_inc(evac, 1)
                act.wait_ge(unit_used, used(l, 7))
                f(qT[:, :, :].rearrange("p a b -> p (a b)"), wide(0), ACT.Copy).then_inc(evac, 1)
                split_up(act, l, 9)

                def relus(hs):
                    for h in hs:
                        act.wait_ge(idx_ready, nth(idx_ready, l, h + 1))
                        if h >= 2:
                            act.wait_ge(relu_used, nth(relu_used, l, h - 1))
                        f(probs[:, h % 2, :], ps[:, 4 + h % 4, 0:384], ACT.Relu).then_inc(relu_done, 1)

                relus(range(0, 4))
                split_up(act, l, 10)
                act.wait_ge(unit_used, used(l, 9))
                f(qk[:, :, :].rearrange("p a b -> p (a b)"), wide(2), ACT.Copy).then_inc(evac, 1)
                relus(range(4, 8))
                split_up(act, l, 11)
                split_up(act, l, 12)
                act.wait_ge(unit_used, used(l, 11))
                f(v_h[:, :, :].rearrange("p a b -> p (a b)"), wide(0), ACT.Copy).then_inc(evac, 1)
                split_up(act, l, 13)
                split_up(act, l, 14)
                act.wait_ge(unit_used, used(l, 13))
                f(v_r[:, :, :].rearrange("p a b -> p (a b)"), wide(2), ACT.Copy).then_inc(evac, 1)
                split_up(act, l, 15)
                split_up(act, l, 16)
                act.wait_ge(unit_used, used(l, 15))
                f(silu_r[:, :, :].rearrange("p a b -> p (a b)"), wide(0), ACT.Sigmoid).then_inc(sgr_ready, 1)
                split_up(act, l, 17)
                split_up(act, l, 18)
                act.wait_ge(unit_used, used(l, 17))
                f(silu_h[:, :, :].rearrange("p a b -> p (a b)"), wide(2), ACT.Sigmoid).then_inc(sgh_ready, 1)

                def gate_job(j):
                    act.wait_ge(unit_used, used(l, U_GT + 2 * j + 2))
                    if j < 3:
                        act.wait_ge(lvl_used, nth(lvl_used, l, 9))
                        act.wait_ge(qkr_ready, nth(qkr_ready, l, 1))
                    f(gates[:, 4 * j:4 * j + 4, :].rearrange("p a b -> p (a b)"), wide(2 * (j % 2)), ACT.Tanh, scale=0.5) \
                        .then_inc(evac, 1)

                def queries_out(r):
                    act.wait_ge(qlat_ps, nth(qlat_ps, l, r + 1))
                    for b in range(2):
                        o = f(qlat[:, 4 * r + b:4 * r + 4:2, :], ps[:, 4 + b, :].rearrange("p (a b) -> p a b", a=2), ACT.Copy, scale=DH ** -0.5)
                    o.then_inc(qlat_ready, 1)

                def exps(h):
                    act.wait_ge(nmax_ready, nth(nmax_ready, l, h + 1))
                    b = h % 2
                    f(probs[:, b, 0:P], probs[:, b, 0:P], ACT.Exp, bias=nmax[:, 2 * b:2 * b + 1], accum_out=rsum[:, 2 * b:2 * b + 1])
                    f(probs[:, b, P:384], probs[:, b, P:384], ACT.Exp, bias=nmax[:, 2 * b + 1:2 * b + 2], accum_out=rsum[:, 2 * b + 1:2 * b + 2]) \
                        .then_inc(exp_done, 1)

                def probs_out(h):
                    act.wait_ge(pT_ps, nth(pT_ps, l, h + 1))
                    if h >= 2:
                        act.wait_ge(pv_done, nth(pv_done, l, h - 1))
                    f(probsT[:, h % 2, :], ps[:, 4 + h % 2, 0:384], ACT.Copy).then_inc(pT_ready, 1)

                split_up(act, l, 19)
                queries_out(0)
                split_up(act, l, 20)
                act.wait_ge(ohg_ready, nth(ohg_ready, l, 1))
                for t in range(TT):
                    o = f(junk[:, 512 * t:512 * (t + 1)], ps[:, 6 + t, :], ACT.Square, accum_out=hss[:, t:t + 1])
                o.then_inc(ohg_sq, 1)
                queries_out(1)
                gate_job(0)
                for g in range(2, 12):
                    split_up(act, l, U_GT + g + 2)
                    if g == 2:
                        act.wait_ge(yretT, nth(yretT, l, 1))
                        f(yret_up[:, :, :].rearrange("p a b -> p (a b)"), wide(4), ACT.Copy).then_inc(yret_upd, 1)
                    if g == 3:
                        gate_job(1)
                        act.wait_ge(yhgT, nth(yhgT, l, 1))
                        for k in range(4):
                            o = f(yhg_up[:, k, :], ps[:, 6 + k // 2, (k % 2) * T:(k % 2 + 1) * T], ACT.Copy, scale=prm[:, Q_HGN + k:Q_HGN + k + 1])
                        o.then_inc(yhg_upd, 1)
                    if g >= 3:
                        if g >= 4:
                            probs_out(g - 4)
                        if g - 3 < HD:
                            exps(g - 3)
                    if g > 3 and g % 2 == 1:
                        gate_job(g // 2)
                split_up(act, l, 31)
                act.wait_ge(pv_done, nth(pv_done, l, HD))
                f(ydsa_up[:, :, :].rearrange("p a b -> p (a b)"), wide(6), ACT.Copy).then_inc(ydsa_upd, 1)
                act.dma_start(gpost[:, :], ln_mix_post[l].partition_broadcast(P)).then_inc(gpost_in, 16)
                for u in range(32, 36):
                    split_up(act, l, u)
                    if u == 33:
                        act.wait_ge(mrg_ready, nth(mrg_ready, l, 1))
                        f(h_up[:, 0:4, :].rearrange("p a b -> p (a b)"), mrg[:, :, :].rearrange("p a b -> p (a b)"), ACT.Copy, scale=0.5) \
                            .then_inc(mrg_up, 1)
                split_up(act, l, 36)
                act.wait_ge(mrg_ready, nth(mrg_ready, l, 2))
                f(h_up[:, 4:8, :].rearrange("p a b -> p (a b)"), mrg[:, :, :].rearrange("p a b -> p (a b)"), ACT.Copy, scale=0.5) \
                    .then_inc(mrg_up, 1)
                for u in range(37, 41):
                    split_up(act, l, u)
                act.wait_ge(unit_used, used(l, U_FF))
                o_stage(0)
                x_stage(1, Q_FFN)
                act.dma_start(gpost[:, :], ln_ffn_post[l].partition_broadcast(P)).then_inc(gpost_in, 16)

                def conv(half, j, n_units, step, c, ready, base_sig):
                    act.drain()
                    act.wait_ge(unit_used, used(l, n_units, step))
                    act.wait_ge(cvp_ready, nth(cvp_ready, l, j + 1))
                    for i in range(2):
                        o = f(c[:, i, :], ps[:, 4 + half, i * T:(i + 1) * T], ACT.Identity,
                              bias=cvp[:, 0, half, i:i + 1], scale=cvp[:, 3, half, i:i + 1])
                    o.then_inc(base_sig, 1)

                def gelu(j):
                    act.wait_ge(cva_done, nth(cva_done, l, j + 1))
                    f(gel[:, :, :], cva[:, :, :], ACT.Gelu_apprx_tanh).then_inc(gel_done, 1)

                def g_upper(j):
                    act.wait_ge(gf_done, nth(gf_done, l, j + 1))
                    f(g_up[:, :, :], gf[:, :, :], ACT.Copy).then_inc(gup_done, 1)

                split_up(act, l, 41)
                conv(0, 0, U_FF + 1, 0, cva, None, cva_base)
                split_up(act, l, 42)
                conv(1, 0, U_FF + 2, 0, cvu, None, cvu_base)
                gelu(0)
                g_upper(0)
                split_up(act, l, 43)
                with act.Fori(0, NPAIR - 2) as j:
                    split_up(act, l, 44, step=j)
                    conv(0, j + 1, U_FF + 3, j, cva, None, cva_base)
                    split_up(act, l, 45, step=j)
                    conv(1, j + 1, U_FF + 4, j, cvu, None, cvu_base)
                    gelu(j + 1)
                    split_up(act, l, 46, step=j)
                    act.wait_ge(unit_used, used(l, U_FF + 5, j))
                    g_upper(j + 1)
                split_up(act, l, UNITS - 1)
                conv(0, NPAIR - 1, UNITS - 3, 0, cva, None, cva_base)
                conv(1, NPAIR - 1, UNITS - 2, 0, cvu, None, cvu_base)
                gelu(NPAIR - 1)
                act.wait_ge(unit_used, used(l, UNITS - 1))
                g_upper(NPAIR - 1)
                act.wait_ge(unit_used, used(l, UNITS))
                o_stage(1)

        @block.vector
        def _(dve):
            v = nc.vector

            def settle():
                dve.drain()

            lb4, rec4, cum4 = small[:, 84:88], small[:, 88:92], small[:, 92:96]
            v.memset(nhalf, -0.5)
            dve.wait_ge(setup_v, 1)
            v.tensor_copy(lb4, prm_all[:, 0, Q_LB:Q_LB + 4])
            settle()
            for i in range(1, DEPTH):
                v.tensor_tensor(lb4, lb4, prm_all[:, i, Q_LB:Q_LB + 4], ALU.max)
                settle()
            for i in range(DEPTH):
                o = v.tensor_tensor(lbs[:, i, 3, :], prm_all[:, i, Q_LB:Q_LB + 4], lb4, ALU.subtract)
            o.then_inc(setup_done, 1)
            dve.wait_ge(setup_v, 2)
            v.tensor_copy(cum4, lbs[:, 0, 2, :])
            settle()
            for i in range(1, DEPTH):
                v.tensor_tensor(cum4, cum4, lbs[:, i, 2, :], ALU.add)
                settle()
            v.reciprocal(rec4, cum4)
            settle()
            for i in range(DEPTH):
                v.tensor_tensor(lbs[:, i, 2, :], lbs[:, i, 2, :], rec4, ALU.mult)
            settle()
            v.tensor_copy(cum4, lbs[:, 0, 2, :])
            settle()
            for i in range(DEPTH):
                if i:
                    v.tensor_tensor(cum4, cum4, lbs[:, i, 2, :], ALU.add)
                    settle()
                v.tensor_tensor(lbs[:, i, 0, :], cum4, lbs[:, 0, 2, :], ALU.subtract)
                settle()
                v.tensor_scalar(lbs[:, i, 0, :], lbs[:, i, 0, :], 0.0, 1.0, ALU.max, ALU.min)
                settle()
                v.tensor_scalar(lbs[:, i, 1, :], lbs[:, i, 0, :], -1.0, 1.0, ALU.mult, ALU.add)
            dve.wait_ge(x_in, 16)

            with dve.Fori(0, DEPTH) as l:
                settle()
                v.tensor_copy(lbc, lbs[:, l, 0:2, :].rearrange("p a b -> p (a b)"))
                v.tensor_copy(prm[:, :], prm_all[:, l, :]).then_inc(prm_ready, 1)

                def lower(u, step=0):
                    split_low(nc.vector, l, u, step)

                def x_stage(stage, g0):
                    for t in range(TT):
                        dve.wait_ge(x_sq, nth(x_sq, l, 2 * stage + t + 1))
                        v.tensor_scalar(ss[:, t:t + 1], ss[:, t:t + 1], 1.0 / D, EPS, ALU.mult, ALU.add).then_inc(n_var, 1)
                    for t in range(TT):
                        dve.wait_ge(n_rs, nth(n_rs, l, 2 * stage + t + 1))
                        v.tensor_scalar(xs[:, t, :], xr[:, t, :], rs[:, t:t + 1], None, ALU.mult).then_inc(xs_ready, 1)
                    for k in range(KD):
                        if k % 2 == 0:
                            dve.wait_ge(h_up_done, nth(h_up_done, l, 4 * stage + k // 2 + 1))
                        o = v.scalar_tensor_tensor(out=h_low[:, k, :], in0=ps[:, 4 + k // 2, (k % 2) * T:(k % 2 + 1) * T],
                                               scalar=prm[:, g0 + k:g0 + k + 1], in1=h_up[:, k, :].bitcast(F32),
                                               op0=ALU.mult, op1=ALU.subtract)
                        if k % 2:
                            o.then_inc(h_low_done, 1)

                def o_stage(stage):
                    for t in range(TT):
                        dve.wait_ge(o_sq, nth(o_sq, l, 2 * stage + t + 1))
                        v.tensor_scalar(oss[:, t:t + 1], oss[:, t:t + 1], 1.0 / D, EPS, ALU.mult, ALU.add).then_inc(o_var, 1)
                    dve.wait_ge(gpost_in, nth(gpost_in, l, 16 * (stage + 1)))
                    for t in range(TT):
                        dve.wait_ge(o_rs, nth(o_rs, l, 2 * stage + t + 1))
                        v.scalar_tensor_tensor(out=xtmp[:, t, :], in0=wide(2 * t), scalar=ors[:, t:t + 1], in1=gpost[:, :],
                                               op0=ALU.mult, op1=ALU.mult)
                        settle()
                        v.tensor_tensor(xr[:, t, :], xr[:, t, :], xtmp[:, t, :], ALU.add).then_inc(x_new, 1)

                x_stage(0, Q_PRE)
                lower(2)
                dve.wait_ge(unit_used, used(l, 2))
                v.tensor_scalar(wi, ps[:, 7, 0:16], 512 ** -0.5, None, ALU.mult).then_inc(wi_ready, 1)
                dve.wait_ge(ss_ready, nth(ss_ready, l, 1))
                v.tensor_scalar(cs4[:, 0:2], ps[:, 7, 32:34], 1.0 / QR, EPS, ALU.mult, ALU.add)
                v.tensor_scalar(cs4[:, 2:4], ps[:, 7, 34:36], 1.0 / KVR, EPS, ALU.mult, ALU.add).then_inc(cvar, 1)
                dve.wait_ge(crs, nth(crs, l, 1))
                for i in range(4):
                    o = v.tensor_scalar(diag[:, i, :], ident, cr4[:, i:i + 1], None, ALU.mult)
                o.then_inc(diag_ready, 1)
                lower(5)
                dve.wait_ge(zs_ready, nth(zs_ready, l, 1))
                dve.wait_ge(bc_ready, nth(bc_ready, l, 1))
                v.tensor_tensor(cqT[:, :, :], zs[:, 0:2, :], ps[:, 6, 0:T].unsqueeze(1).to_broadcast([P, 2, T]), ALU.mult)
                v.tensor_tensor(ckvT[:, :], zs[:, 2, :], ps[:, 6, T:2 * T], ALU.mult)
                settle()
                v.tensor_copy(cq_up[:, :, :], cqT[:, :, :])
                settle()
                v.tensor_tensor(cq_low[:, :, :], cqT[:, :, :], cq_up[:, :, :].bitcast(F32), ALU.subtract).then_inc(c_ready, 1)
                dve.wait_ge(evac, nth(evac, l, 2))
                for h in range(HG):
                    c = slice(h * T, (h + 1) * T)
                    v.tensor_scalar(hgf[:, c], hgf[:, c], lbc[:, 4 + h:5 + h], lbc[:, h:h + 1], ALU.mult, ALU.add)
                    v.tensor_scalar(hgk[:, c], hgk[:, c], lbc[:, 4 + h:5 + h], None, ALU.mult)
                settle()
                v.tensor_scalar(hgf[:, :], hgf[:, :], FLOOR, None, ALU.max).then_inc(fk_ready, 1)
                lower(8)
                for h in range(HD):
                    dve.wait_ge(relu_done, nth(relu_done, l, h + 1))
                    for t, c in ((0, slice(0, P)), (1, slice(P, 384))):
                        w = wi[:, 8 * t + h:8 * t + h + 1]
                        if h == 0:
                            o = v.tensor_scalar(score[:, c], probs[:, 0, c], w, 0.0, ALU.mult, ALU.add)
                        else:
                            o = v.scalar_tensor_tensor(out=score[:, c], in0=probs[:, h % 2, c], scalar=w, in1=score[:, c],
                                                       op0=ALU.mult, op1=ALU.add)
                    o.then_inc(relu_used, 1)
                    settle()
                v.tensor_tensor(score[:, :], score[:, :], cmask, ALU.add)
                settle()
                lower(11)

                def top_round():
                    for t, c in ((0, slice(0, P)), (1, slice(P, 384))):
                        v.max(best8[:, 8 * t:8 * t + 8], score[:, c])
                    settle()
                    for t, c in ((0, slice(0, P)), (1, slice(P, 384))):
                        v.match_replace(score[:, c], best8[:, 8 * t:8 * t + 8], score[:, c], TAKEN)
                    settle()

                def hgrn_step(n):
                    settle()
                    dve.wait_ge(lvl_ready, nth(lvl_ready, l, n + 2))
                    if n == -1:
                        v.tensor_tensor(hgq[:, :], hgq[:, :], hgf[:, :], ALU.mult).then_inc(lvl_next, 1)
                        v.tensor_tensor(att[:, :, :], ps[:, 6:8, :].rearrange("p a (b c) -> p (a b) c", c=P),
                                        ident.unsqueeze(1).to_broadcast([P, 8, P]), ALU.mult).then_inc(lvl_used, 1)
                        return
                    if n == LEVELS:
                        v.tensor_copy(att2[:, :, :].rearrange("p a b -> p (a b)"), ps[:, 6 + n % 2, :]).then_inc(lvl_used, 1)
                        return
                    m = 1 << n
                    now, nxt = (hgf, hgf2) if n % 2 == 0 else (hgf2, hgf)
                    g = now[:, 0:HG * T // m].rearrange("p (x two) -> p x two", two=2)
                    q = hgq[:, :].rearrange("p (x two m) -> p x two m", two=2, m=m)
                    k = hgk[:, :].rearrange("p (x two m) -> p x two m", two=2, m=m)
                    nx = HG * T // (2 * m)
                    v.tensor_tensor(q[:, :, 1, :], q[:, :, 1, :], g[:, :, 0:1].to_broadcast([P, nx, m]), ALU.mult)
                    v.tensor_tensor(k[:, :, 0, :], k[:, :, 0, :], g[:, :, 1:2].to_broadcast([P, nx, m]), ALU.mult).then_inc(lvl_next, 1)
                    if n < LEVELS - 1:
                        v.tensor_tensor(nxt[:, 0:nx], g[:, :, 0], g[:, :, 1], ALU.mult)
                    v.copy_predicated(
                        att[:, :, :].rearrange("p a (b two m) -> p a b two m", two=2, m=m)[:, :, :, 1, :],
                        kc[:, K_LV + 64 * n:K_LV + 64 * n + 64].bitcast(U32).rearrange("p (b m) -> p b m", m=m).unsqueeze(1)
                        .to_broadcast([P, 8, 64 // m, m]),
                        ps[:, 6 + n % 2, :].rearrange("p (a b m) -> p a b m", a=8, m=m)).then_inc(lvl_used, 1)

                dve.wait_ge(evac, nth(evac, l, 6))
                v.tensor_tensor(qkcos[:, :, :], qk[:, :, :], cos.unsqueeze(1).to_broadcast([P, 4, T]), ALU.mult)
                hgrn_step(-1)
                dve.wait_ge(rot_ready, nth(rot_ready, l, 1))
                v.tensor_tensor(qkr[:, :, :], ps[:, 4:6, :].rearrange("p a (b c) -> p (a b) c", c=T),
                                sin.unsqueeze(1).to_broadcast([P, 4, T]), ALU.mult)
                settle()
                v.tensor_tensor(qkr[:, :, :], qkr[:, :, :], qkcos[:, :, :], ALU.add).then_inc(qkr_ready, 1)

                def decay(h):
                    dve.wait_ge(dot_ready, nth(dot_ready, l, h + 1))
                    dm = kc[:, K_DM + h * T:K_DM + (h + 1) * T]
                    v.tensor_tensor(dec[:, h, 0:T], ps[:, 4 + h % 2, 0:T], dm, ALU.mult)
                    v.tensor_tensor(dec[:, h, T:T + P], ps[:, 4 + h % 2, T:T + P], dm[:, 0:P], ALU.mult).then_inc(dec_ready, 1)

                def gated(s, b, sig_in, sig_out):
                    dve.wait_ge(sig_in, nth(sig_in, l, 1))
                    sv = s[:, :, :].rearrange("p a b -> p (a b)")
                    v.tensor_tensor(sv, sv, wide(b), ALU.mult).then_inc(sig_out, 1)

                top_round()
                hgrn_step(0)
                hgrn_step(1)
                decay(0)
                decay(1)
                top_round()
                lower(14)
                hgrn_step(2)
                decay(2)
                decay(3)
                top_round()
                hgrn_step(3)
                dve.wait_ge(oret_ready, nth(oret_ready, l, 1))
                for a in range(8):
                    v.bn_stats(bn6[:, a, :], ps[:, 4 + a // 4, (a % 4) * P:(a % 4 + 1) * P])
                settle()
                for a in range(8):
                    v.bn_aggr(bna[:, a, :], bn6[:, a, :])
                settle()
                v.tensor_scalar(bnr, bna[:, :, 1], EPS, None, ALU.add).then_inc(bn_var, 1)
                top_round()
                hgrn_step(4)
                gated(silu_r, 0, sgr_ready, silur_ready)
                lower(17)
                top_round()
                hgrn_step(5)
                dve.wait_ge(bn_rs, nth(bn_rs, l, 1))
                for a in range(8):
                    v.tensor_scalar(yn_r[:, a // 4, (a % 4) * P:(a % 4 + 1) * P], ps[:, 4 + a // 4, (a % 4) * P:(a % 4 + 1) * P],
                                    bna[:, a, 0:1], bnr2[:, a:a + 1], ALU.subtract, ALU.mult)
                settle()
                v.tensor_tensor(yn_r[:, :, :], yn_r[:, :, :], silu_r[:, :, :], ALU.mult).then_inc(ynr_ready, 1)
                top_round()
                hgrn_step(6)
                gated(silu_h, 2, sgh_ready, siluh_ready)
                lower(20)
                top_round()
                top_round()
                v.tensor_scalar(score[:, :], score[:, :], -2e38, NEG, ALU.is_gt, ALU.mult)
                settle()
                v.tensor_tensor(score[:, :], score[:, :], cmask, ALU.min).then_inc(chosen, 1)
                hgrn_step(7)
                dve.wait_ge(ohg_sq, nth(ohg_sq, l, 1))
                v.tensor_scalar(hss, hss, 1.0 / 512, EPS, ALU.mult, ALU.add).then_inc(ohg_var, 1)
                dve.wait_ge(ohg_rs, nth(ohg_rs, l, 1))
                for t in range(TT):
                    o = v.scalar_tensor_tensor(out=yn_h[:, t, :], in0=ps[:, 6 + t, :], scalar=hrs[:, t:t + 1], in1=silu_h[:, t, :],
                                               op0=ALU.mult, op1=ALU.mult)
                o.then_inc(ynh_ready, 1)
                dve.wait_ge(yret_upd, nth(yret_upd, l, 1))
                v.tensor_tensor(yret_low[:, :, :].rearrange("p a b -> p (a b)"), wide(4),
                                yret_up[:, :, :].bitcast(F32).rearrange("p a b -> p (a b)"), ALU.subtract).then_inc(yret_done, 1)
                dve.wait_ge(yhg_upd, nth(yhg_upd, l, 1))
                for k in range(4):
                    o = v.scalar_tensor_tensor(out=yhg_low[:, k, :], in0=ps[:, 6 + k // 2, (k % 2) * T:(k % 2 + 1) * T],
                                               scalar=prm[:, Q_HGN + k:Q_HGN + k + 1], in1=yhg_up[:, k, :].bitcast(F32),
                                               op0=ALU.mult, op1=ALU.subtract)
                o.then_inc(yhg_done, 1)
                for h in range(HD):
                    b = h % 2
                    dve.wait_ge(lg_ready, nth(lg_ready, l, h + 1))
                    dve.wait_ge(mb_ready, nth(mb_ready, l, h + 1))
                    if h >= 2:
                        dve.wait_ge(pT_ps, nth(pT_ps, l, h - 1))
                    dve.sem_inc(lg_seen, 1)
                    for t, c in ((0, slice(0, P)), (1, slice(P, 384))):
                        v.tensor_tensor_reduce(probs[:, b, c], ps[:, 4 + b, c], mbias[:, b, c], 1.0, TAKEN, ALU.add, ALU.max,
                                               nmax[:, 2 * b + t:2 * b + t + 1])
                    settle()
                    v.tensor_scalar(nmax[:, 2 * b:2 * b + 2], nmax[:, 2 * b:2 * b + 2], -1.0, None, ALU.mult).then_inc(nmax_ready, 1)
                    if h % 3 == 1:
                        lower(23 + 3 * (h // 3))
                    dve.wait_ge(exp_done, nth(exp_done, l, h + 1))
                    v.reciprocal(rrec[:, 2 * b:2 * b + 2], rsum[:, 2 * b:2 * b + 2])
                    settle()
                    v.tensor_scalar(probs[:, b, 0:P], probs[:, b, 0:P], rrec[:, 2 * b:2 * b + 1], None, ALU.mult)
                    v.tensor_scalar(probs[:, b, P:384], probs[:, b, P:384], rrec[:, 2 * b + 1:2 * b + 2], None, ALU.mult) \
                        .then_inc(prob_ready, 1)
                dve.wait_ge(ydsa_upd, nth(ydsa_upd, l, 1))
                v.tensor_tensor(ydsa_low[:, :, :].rearrange("p a b -> p (a b)"), wide(6),
                                ydsa_up[:, :, :].bitcast(F32).rearrange("p a b -> p (a b)"), ALU.subtract).then_inc(ydsa_done, 1)
                lower(32)
                for nb in range(2):
                    for b in range(3):
                        j = 3 * nb + b
                        dve.wait_ge(unit_used, used(l, U_BR + j + 1))
                        gb = 8 * (0, 2, 1)[b] + 4 * nb
                        gt = gates[:, gb:gb + 4, :].rearrange("p a b -> p (a b)")
                        dst = (mtmp if b else mrg)[:, :, :].rearrange("p a b -> p (a b)")
                        if b == 0 and nb == 1:
                            dve.wait_ge(mrg_up, nth(mrg_up, l, 1))
                        v.scalar_tensor_tensor(out=dst, in0=gt, scalar=1.0, in1=wide(2 * (j % 2)), op0=ALU.add, op1=ALU.mult) \
                            .then_inc(br_used, 1)
                        settle()
                        if b:
                            o = v.tensor_tensor(mrg[:, :, :], mrg[:, :, :], mtmp[:, :, :], ALU.add)
                            if b == 2:
                                o.then_inc(mrg_ready, 1)
                            settle()
                        if j == 3:
                            lower(35)
                    dve.wait_ge(mrg_up, nth(mrg_up, l, nb + 1))
                    v.scalar_tensor_tensor(out=h_low[:, 4 * nb:4 * nb + 4, :], in0=mrg[:, :, :], scalar=0.5,
                                           in1=h_up[:, 4 * nb:4 * nb + 4, :].bitcast(F32), op0=ALU.mult, op1=ALU.subtract) \
                        .then_inc(mrg_done, 1)
                    settle()
                lower(38)
                lower(40)
                o_stage(0)
                x_stage(1, Q_FFN)

                taps = prm[:, Q_CB:NPRM].rearrange("p (w g j n) -> p w g j n", w=4, g=2, n=2)

                def conv_params(j):
                    settle()
                    v.tensor_copy(cvp[:, :, :, :], taps[:, :, :, j, :]).then_inc(cvp_ready, 1)

                def conv(half, j, c, base_sig, done):
                    dve.wait_ge(base_sig, nth(base_sig, l, j + 1))
                    for d in (1, 2):
                        for i in range(2):
                            o = v.scalar_tensor_tensor(out=c[:, i, d:T], in0=ps[:, 4 + half, i * T:(i + 1) * T - d],
                                                       scalar=cvp[:, 3 - d, half, i:i + 1], in1=c[:, i, d:T],
                                                       op0=ALU.mult, op1=ALU.add)
                        if d == 1:
                            settle()
                    o.then_inc(done, 1)

                def gated_up(j):
                    settle()
                    dve.wait_ge(gel_done, nth(gel_done, l, j + 1))
                    v.tensor_tensor(gf[:, :, :], gel[:, :, :], cvu[:, :, :], ALU.mult).then_inc(gf_done, 1)

                def g_lower(j):
                    dve.wait_ge(gup_done, nth(gup_done, l, j + 1))
                    v.tensor_tensor(g_low[:, :, :], gf[:, :, :], g_up[:, :, :].bitcast(F32), ALU.subtract).then_inc(glow_done, 1)

                conv_params(0)
                lower(41)
                conv(0, 0, cva, cva_base, cva_done)
                conv(1, 0, cvu, cvu_base, cvu_done)
                conv_params(1)
                gated_up(0)
                g_lower(0)
                lower(43)
                with dve.Fori(0, NPAIR - 2) as j:
                    lower(44, j)
                    conv(0, j + 1, cva, cva_base, cva_done)
                    conv(1, j + 1, cvu, cvu_base, cvu_done)
                    conv_params(j + 2)
                    gated_up(j + 1)
                    lower(46, j)
                    g_lower(j + 1)
                lower(UNITS - 1)
                conv(0, NPAIR - 1, cva, cva_base, cva_done)
                conv(1, NPAIR - 1, cvu, cvu_base, cvu_done)
                gated_up(NPAIR - 1)
                g_lower(NPAIR - 1)
                o_stage(1)

        @block.gpsimd
        def _(pool):
            pw = nc.gpsimd.tensor_tensor
            for s in low_done:
                pool.sem_inc(s, 1)
            pool.sem_inc(unit_used, SLOTS)

            with pool.Fori(0, DEPTH) as l:
                def lower(u, step=0):
                    split_low(nc.gpsimd, l, u, step)

                def rsqrt(o, i, n, wait, k, done):
                    pool.wait_ge(wait, nth(wait, l, k))
                    pw(o, i, nhalf[:, 0:n], ALU.pow).then_inc(done, 1)

                def stats(i, o, wait, done, stage):
                    for t in range(TT):
                        rsqrt(o[:, t:t + 1], i[:, t:t + 1], 1, wait, 2 * stage + t + 1, done)

                lower(0)
                stats(ss, rs, n_var, n_rs, 0)
                lower(1)
                lower(3)
                rsqrt(cr4, cs4, 4, cvar, 1, crs)
                for u in range(4, 17):
                    if pool_low[u % SLOTS]:
                        lower(u)
                    if u == 14:
                        rsqrt(bnr2, bnr, 8, bn_var, 1, bn_rs)

                def masked_bias(h):
                    b = h % 2
                    if h == 0:
                        pool.wait_ge(chosen, nth(chosen, l, 1))
                        pool.wait_ge(bias_in, 16)
                    if h >= 2:
                        pool.wait_ge(nmax_ready, nth(nmax_ready, l, h - 1))
                    pw(mbias[:, b, 0:P], score[:, 0:P], bias[:, h, P:T], ALU.add)
                    pw(mbias[:, b, P:384], score[:, P:384], bias[:, h, :], ALU.add).then_inc(mb_ready, 1)

                for u in range(17, 40):
                    if pool_low[u % SLOTS] if u < U_FF else pool_low_ffn[u % SLOTS]:
                        lower(u)
                    if u == 18:
                        rsqrt(hrs, hss, 2, ohg_var, 1, ohg_rs)
                    if u == 19:
                        masked_bias(0)
                    if 20 <= u < 27:
                        masked_bias(u - 19)
                stats(oss, ors, o_var, o_rs, 0)
                stats(ss, rs, n_var, n_rs, 1)
                lower(42)
                with pool.Fori(0, NPAIR - 2) as j:
                    lower(45, j)
                stats(oss, ors, o_var, o_rs, 1)


_INS = ["x", "rel_bias", "hgrn_lb", "ln_mix_pre", "ln_mix_post", "ln_ffn_pre", "ln_ffn_post", "w_in",
        "dsa_q_norm", "dsa_kv_norm", "dsa_w_uq", "dsa_w_uk", "dsa_w_uv", "hgrn_norm",
        "w_br_ret", "w_br_dsa", "w_br_hgrn", "w_out", "ffn_w_up", "ffn_conv_w", "ffn_conv_b", "ffn_w_down"]


def kernel(**inputs):
    import concourse.bacc as bacc
    from concourse.bass_utils import run_bass_kernel_spmd

    nc = bacc.Bacc("TRN2", target_bir_lowering=False, num_devices=1)
    arrays = {"shape_constants": shape_constants()}
    arrays.update({f"in_{n}": np.ascontiguousarray(inputs[n]) for n in _INS})
    args = [nc.dram_tensor(n, a.shape, mybir.dt.from_np(a.dtype), kind="ExternalInput").ap() for n, a in arrays.items()]
    y = nc.dram_tensor("y", (1, T, D), F32, kind="ExternalOutput").ap()
    trunk(nc, *args, y)
    return run_bass_kernel_spmd(nc, [arrays], core_ids=[0]).results[0]["y"]
```

```python
from contextlib import ExitStack

import numpy as np

import concourse.bass as bass
from concourse import mybir

ALU = mybir.AluOpType
ACT = mybir.ActivationFunctionType
F32 = mybir.dt.float32
F32R = mybir.dt.float32r
U32 = mybir.dt.uint32

P = 128
T = 256
TT = T // P
D = 1024
KD = D // P
HR, DKR = 4, 64
HD, DH, QR, KVR = 8, 64, 256, 128
TOPK = 64
BIAS_ROWS = 32
HG = 4
DFF = 2816
NPAIR = DFF // (2 * P)
EPS = 1e-6
FLOOR = 1e-6
NEG = -1e30
TAKEN = -3e38
UNIT = 2048
SLOTS = 3
LEVELS = 7

C_RQ, C_RK, C_RV, C_RG = 0, 256, 512, 1024
C_CQ, C_KV = 1536, 1792
C_HQ, C_HF, C_HV, C_HG, C_GT = 1992, 2504, 3016, 3528, 4040

U_CQ, U_KV, U_HF, U_HQ, U_UQ, U_RQ, U_RK = 0, 1, 2, 4, 6, 7, 8
U_HV, U_RV, U_RG, U_HGATE, U_GT, U_BR, U_WO, U_FF = 9, 11, 13, 15, 17, 29, 35, 39
UNITS = U_FF + 3 * NPAIR
PER_SLOT = UNITS // SLOTS
assert UNITS % SLOTS == 0

Q_PRE, Q_FFN, Q_QN, Q_KVN, Q_HGN, Q_LB, Q_CB, Q_CW = 0, 8, 16, 18, 19, 23, 27, 71
NPRM = Q_CW + 3 * 44

K_ID, K_ROT, K_ONE, K_COS, K_SIN, K_DM, K_CM, K_LV, K_OH = 0, 128, 256, 384, 640, 896, 1920, 2304, 2752
K_ALL = K_OH + 384
K_MAT = K_ONE + P


def shape_constants():
    f = np.float32
    k = np.zeros((P, K_ALL), f)
    i = np.arange(P)
    k[:, K_ID:K_ID + P] = np.eye(P)
    for d in range(P):
        if d % 64 < 32:
            k[d + 32, K_ROT + d] = -1.0
        else:
            k[d - 32, K_ROT + d] = 1.0
    k[:, K_ONE:K_ONE + P] = 1.0
    freq = (f(1.0) / np.power(f(10000.0), np.linspace(0.0, 1.0, 32, dtype=f))).astype(f)
    ang = (np.arange(T, dtype=f)[None, :] * freq[i % 32][:, None]).astype(f)
    k[:, K_COS:K_COS + T] = np.cos(ang)
    k[:, K_SIN:K_SIN + T] = np.sin(ang)
    log_gamma = np.log1p(-(2.0 ** (-5.0 - np.arange(HR))))
    rel = np.arange(T)[None, :] - i[:, None]
    for h in range(HR):
        k[:, K_DM + h * T:K_DM + (h + 1) * T] = np.where(rel >= 0, np.exp(np.maximum(rel, 0) * log_gamma[h]), 0) * DKR ** -0.5
    k[:, K_CM:K_CM + P] = np.where(i[None, :] <= i[:, None], 0.0, NEG)
    k[:, K_CM + P:K_CM + 3 * P] = np.where(np.arange(T)[None, :] <= P + i[:, None], 0.0, NEG)
    for v in range(LEVELS):
        m = 1 << v
        for c in range(64):
            b = c // m
            k[2 * b * m:(2 * b + 1) * m, K_LV + 64 * v + c] = 1.0
    n = np.maximum(256 - np.arange(384), 0)
    nf = np.maximum(n, 16).astype(f)
    large = 16 + (np.log(nf / f(16)) / f(np.log(8.0)) * f(16)).astype(np.int32)
    bucket = np.where(n < 16, n, np.minimum(large, 31))
    k[bucket, K_OH + np.arange(384)] = 1.0
    return k


def trunk(nc, consts, params, x, rel_bias, ln_mix_post, ln_ffn_post, w_in,
          dsa_w_uq, dsa_w_uk, dsa_w_uv, w_br_ret, w_br_dsa, w_br_hgrn, w_out, ffn_w_up, ffn_w_down, out):
    DEPTH = w_in.shape[0]
    scratch = nc.dram_tensor("bias_rows", (BIAS_ROWS, HD, 384), F32, kind="Internal").ap()

    with ExitStack() as ctx:
        ARENA = 53200 * 4
        ctx.enter_context(nc.sbuf_tensor("arena", [P, ARENA // 4], F32))
        base = 16512
        here = [base]

        def at(name, offset, shape, dt=F32):
            return nc.alloc_sbuf_tensor_at(name, shape, dt, offset=offset)

        def keep(name, shape, dt=F32):
            n = 4
            for s in shape[1:]:
                n *= s
            o = here[0]
            here[0] += (n + 31) // 32 * 32
            return at(name, o, shape, dt)

        def room(nbytes):
            o = here[0]
            here[0] += nbytes
            return o

        kc = keep("kc", [P, K_OH])
        raw = [keep(f"raw{i}", [P, UNIT]) for i in range(SLOTS)]
        up = [keep(f"up{i}", [P, UNIT], F32R) for i in range(SLOTS)]
        low = [keep(f"low{i}", [P, UNIT], F32R) for i in range(SLOTS)]
        xr = keep("xr", [P, TT, D])
        h_up = keep("h_up", [P, KD, T], F32R)
        h_low = keep("h_low", [P, KD, T], F32R)
        bias = keep("bias", [P, HD, T])
        prm_all = keep("prm_all", [P, DEPTH, NPRM])
        prm = keep("prm", [P, NPRM])
        lbs = keep("lbs", [P, DEPTH, 4, 4])
        w_uk = keep("w_uk", [P, 4, P])
        w_uv = keep("w_uv", [P, HD, DH])
        r_gate, r_dsa, r_hg, r_ret = room(24 * 1024), room(8 * 1024), room(8 * 1024), room(8 * 1024)
        gates = at("gates", r_gate, [P, 24, T])
        xs = at("xs", r_gate, [P, TT, D])
        junk = at("junk", r_gate + 8192, [P, D])
        hgq = at("hgq", r_gate, [P, HG * T])
        hgk = at("hgk", r_gate + 4096, [P, HG * T])
        hgf = at("hgf", r_gate + 8192, [P, HG * T])
        qk = at("qk", r_gate + 12288, [P, 4, T])
        qkcos = at("qkcos", r_gate + 16384, [P, 4, T])
        qkr = at("qkr", r_gate + 20480, [P, 4, T])
        ydsa_up = at("ydsa_up", r_dsa, [P, 4, T], F32R)
        ydsa_low = at("ydsa_low", r_dsa + 4096, [P, 4, T], F32R)
        zs = at("zs", r_dsa, [P, 3, T])
        ikT = at("ikT", r_dsa + 3072, [P, T])
        iwT = at("iwT", r_ret + 1536, [P, T])
        cq_up = at("cq_up", r_dsa + 4096, [P, 2, T], F32R)
        cq_low = at("cq_low", r_dsa + 6144, [P, 2, T], F32R)
        silu_h = at("silu_h", r_dsa, [P, TT, 512])
        silu_r = at("silu_r", r_dsa + 4096, [P, TT, 512])
        yhg_up = at("yhg_up", r_hg, [P, 4, T], F32R)
        yhg_low = at("yhg_low", r_hg + 4096, [P, 4, T], F32R)
        sq = at("sq", r_hg, [P, 3, T])
        qiT = at("qiT", r_hg + 4096, [P, 4, T])
        att = at("att", r_hg, [P, 8, P])
        att2 = at("att2", r_hg + 4096, [P, HG, P])
        yret_up = at("yret_up", r_ret, [P, 4, T], F32R)
        yret_low = at("yret_low", r_ret + 4096, [P, 4, T], F32R)
        qT = at("qT", r_ret, [P, 4, T])
        r_tmp = here[0]
        ckvT = at("ckvT", r_tmp, [P, T])
        cqT = at("cqT", r_tmp + 1024, [P, 2, T])
        vlat = at("vlat", r_tmp + 3072, [P, TT, HD * DH])
        probs = at("probs", r_tmp + 7168, [P, 2, 384])
        score = at("score", r_tmp + 10240, [P, 384])
        mbias = at("mbias", r_tmp + 11776, [P, 2, 384])
        probsT = at("probsT", r_tmp + 14848, [P, 2, 384])
        v_h = at("v_h", r_tmp + 17920, [P, TT, 512])
        v_r = at("v_r", r_tmp + 22016, [P, TT, 512])
        yn_r = v_r
        yn_h = v_h
        dec = at("dec", r_tmp + 26112, [P, HR, 384])
        qlat = at("qlat", r_tmp + 26112, [P, HD, T])
        diag = at("diag", r_tmp + 26112, [P, 4, P])
        hgf2 = at("hgf2", r_tmp + 34304, [P, 512])
        small = at("small", r_tmp + 36352, [P, 192])
        mrg = at("mrg", r_tmp + 17920, [P, 4, T])
        mtmp = at("mtmp", r_tmp + 22016, [P, 4, T])
        og = at("og", r_tmp + 17920, [P, TT, D])
        gpost = at("gpost", r_tmp + 26112, [P, D])
        cva = at("cva", r_tmp, [P, 2, T])
        cvu = at("cvu", r_tmp + 2048, [P, 2, T])
        gel = at("gel", r_tmp + 4096, [P, 2, T])
        gf = at("gf", r_tmp + 6144, [P, 2, T])
        g_up = at("g_up", r_tmp + 8192, [P, 2, T], F32R)
        g_low = at("g_low", r_tmp + 10240, [P, 2, T], F32R)
        g_last = [at("g_up_last", r_tmp + 12544, [P, 2, T], F32R), at("g_low_last", r_tmp + 14592, [P, 2, T], F32R)]
        cvp = at("cvp", r_tmp + 12288, [P, 4, 2, 2])
        onehot = at("onehot", r_hg, [P, 384])
        relb = at("relb", r_hg + 1536, [P, HD])
        brow = at("brow", r_ret, [P, 384])
        assert r_tmp + 37000 <= base + ARENA, (r_tmp + 37000, base + ARENA)

        ident, rot = kc[:, K_ID:K_ID + P], kc[:, K_ROT:K_ROT + P]
        ones, cos, sin = kc[:, K_ONE:K_ONE + P], kc[:, K_COS:K_COS + T], kc[:, K_SIN:K_SIN + T]
        cmask = kc[:, K_CM:K_CM + 384]
        nhalf, ss, rs = small[:, 0:8], small[:, 8:16], small[:, 16:24]
        cs4, cr4, wi = small[:, 24:28], small[:, 28:32], small[:, 32:48]
        oss, ors, best8 = small[:, 48:52], small[:, 52:56], small[:, 56:72]
        nmax, rsum, rrec = small[:, 72:76], small[:, 76:80], small[:, 80:84]
        bn6 = small[:, 84:132].rearrange("p (a b) -> p a b", b=6)
        bna = small[:, 132:148].rearrange("p (a b) -> p a b", b=2)
        bnr = small[:, 148:156]
        bnr2, lbc = small[:, 160:168], small[:, 168:176]
        hss = small[:, 156:158]
        hrs = small[:, 158:160]

        ps = ctx.enter_context(nc.psum_tensor("ps", [P, 8, 512], F32))

        def wide(b):
            return ps[:, b:b + 2, :].rearrange("p a b -> p (a b)")

        per_layer = {}

        def sig(name, per):
            s = ctx.enter_context(nc.semaphore(name))
            per_layer[s.name] = per
            return s

        def nth(signal, layer, k):
            return layer * per_layer[signal.name] + k

        raw_in = [sig(f"raw_in{i}", 16 * PER_SLOT) for i in range(SLOTS)]
        up_done = sig("up_done", UNITS)
        low_done = [sig(f"low_done{i}", PER_SLOT) for i in range(SLOTS)]
        unit_used = sig("unit_used", UNITS)
        setup_in, setup_ps, setup_cp, bias_out, setup_done, setup_v = (
            sig(n, 1) for n in ("setup_in", "setup_ps", "setup_cp", "bias_out", "setup_done", "setup_v"))
        bias_in = sig("bias_in", 16 * P // BIAS_ROWS)
        prm_ready, prm_in, masks_in = sig("prm_ready", 1), sig("prm_in", 16), sig("masks_in", 16)
        small_in = sig("small_in", 32)
        x_sq, n_var, n_rs, xs_ready = sig("x_sq", 4), sig("n_var", 4), sig("n_rs", 4), sig("xs_ready", 4)
        xT_ready, h_up_done, h_low_done = sig("xT_ready", 8), sig("h_up_done", 8), sig("h_low_done", 16)
        og_half, o_sq_half = sig("og_half", 4), sig("o_sq_half", 4)
        o_ready, o_sq, o_var, o_rs, x_new = sig("o_ready", 2), sig("o_sq", 4), sig("o_var", 4), sig("o_rs", 4), sig("x_new", 4)
        gpost_in = sig("gpost_in", 32)
        evac = sig("evac", 14)
        wi_ps, sq_ready, zs_ready, ss_ready, cvar, crs, diag_ready, bc_ready, c_ready = (
            sig(n, 1) for n in ("wi_ps", "sq_ready", "zs_ready", "ss_ready", "cvar", "crs", "diag_ready", "bc_ready", "c_ready"))
        v_ready, vlat_ready, uqi_ready = sig("v_ready", 1), sig("vlat_ready", 1), sig("uqi_ready", 1)
        idx_ready, relu_done, relu_used = sig("idx_ready", HD), sig("relu_done", HD), sig("relu_used", HD)
        low_head = sig("low_head", 1)
        slot_seen = sig("slot_seen", UNITS)
        ik_twice = sig("ik_twice", 16)
        chosen = sig("chosen", 1)
        fk_ready = sig("fk_ready", 1)
        lvl_ready, lvl_next, lvl_used = sig("lvl_ready", 9), sig("lvl_next", 8), sig("lvl_used", 9)
        rot_ready, qkr_ready, dot_ready, dec_ready = sig("rot_ready", 1), sig("qkr_ready", 1), sig("dot_ready", HR), sig("dec_ready", HR)
        oret_ready, bn_var, bn_rs, ynr_ready = sig("oret_ready", 1), sig("bn_var", 1), sig("bn_rs", 1), sig("ynr_ready", 1)
        ohg_ready, ohg_sq, ohg_var, ohg_rs, ynh_ready = (sig(n, 1) for n in ("ohg_ready", "ohg_sq", "ohg_var", "ohg_rs", "ynh_ready"))
        sgr_ready, silur_ready, sgh_ready, siluh_ready = (sig(n, 1) for n in ("sgr_ready", "silur_ready", "sgh_ready", "siluh_ready"))
        yretT, yret_upd, yret_done, yhgT, yhg_upd, yhg_done, ydsa_upd, ydsa_done = (
            sig(n, 1) for n in ("yretT", "yret_upd", "yret_done", "yhgT", "yhg_upd", "yhg_done", "ydsa_upd", "ydsa_done"))
        qlat_ps, qlat_ready = sig("qlat_ps", 2), sig("qlat_ready", 2)
        mb_ready, lg_ready, lg_seen, nmax_ready, exp_done, prob_ready, pT_ps, pT_ready, pv_done = (
            sig(n, HD) for n in ("mb_ready", "lg_ready", "lg_seen", "nmax_ready", "exp_done", "prob_ready", "pT_ps", "pT_ready", "pv_done"))
        br_used, mrg_ready, mrg_up, mrg_done = sig("br_used", 6), sig("mrg_ready", 2), sig("mrg_up", 2), sig("mrg_done", 2)
        cvp_ready, cva_base, cvu_base, cva_done, cvu_done, gel_done, gf_done, gup_done, glow_done = (
            sig(n, NPAIR) for n in ("cvp_ready", "cva_base", "cvu_base", "cva_done", "cvu_done", "gel_done", "gf_done", "gup_done", "glow_done"))
        x_in, y_out = [sig(f"x_in{t}", 16) for t in range(TT)], sig("y_out", 16)

        pool_low = [True, True, False]
        pool_low_ffn = [True, False, False]

        def load_unit(sp, l, u, src, step=0):
            s = u % SLOTS
            sp.wait_ge(low_done[s], l * PER_SLOT + u // SLOTS + step + 1)
            sp.sem_inc(slot_seen, 1)
            sp.dma_start(raw[s][:, :].rearrange("p (a b) -> p a b", a=src.shape[1]), src).then_inc(raw_in[s], 16)

        def split_up(act, l, u, step=0):
            s = u % SLOTS
            act.wait_ge(raw_in[s], 16 * (l * PER_SLOT + u // SLOTS + step + 1))
            act.wait_ge(unit_used, l * UNITS + u + SLOTS * step + 1)
            nc.scalar.activation(up[s][:, :], raw[s][:, :], ACT.Copy).then_inc(up_done, 1)

        def split_low(eng, l, u, step=0):
            s = u % SLOTS
            eng.wait_ge(up_done, l * UNITS + u + SLOTS * step + 1)
            eng.tensor_tensor(low[s][:, :], raw[s][:, :], up[s][:, :].bitcast(F32), ALU.subtract).then_inc(low_done[s], 1)

        def lower_share(l, share, eng, done):
            c = (slice(0, 5 * UNIT // 8), slice(5 * UNIT // 8, UNIT))[share]
            eng.wait_ge(up_done, l * UNITS + 1)
            eng.tensor_tensor(low[0][:, c], raw[0][:, c], up[0][:, c].bitcast(F32), ALU.subtract).then_inc(done, 1)

        def fill(l, u, step=0):
            return l * PER_SLOT + u // SLOTS + step + 2

        def used(l, k, step=0):
            return l * UNITS + k + SLOTS * step + SLOTS

        block = ctx.enter_context(nc.Block())

        @block.sync
        def _(sp):
            sp.dma_start(xr[:, 0, :], x[0, 0:P, :]).then_inc(x_in[0], 16)
            sp.dma_start(relb[0:32, :], rel_bias).then_inc(setup_in, 16)
            sp.dma_start(onehot[:, :], consts[:, K_OH:K_ALL]).then_inc(setup_in, 16)
            sp.dma_start(xr[:, 1, :], x[0, P:T, :]).then_inc(x_in[1], 16)

            win = w_in.rearrange("l (k p) n -> l p k n", p=P)
            uqv = dsa_w_uq.rearrange("l (k p) n -> l p k n", p=P)
            wov = w_out.rearrange("l (k p) n -> l p k n", p=P)
            brv = [w.rearrange("l (k p) n -> l p k n", p=P) for w in (w_br_ret, w_br_hgrn, w_br_dsa)]
            ukv = dsa_w_uk.rearrange("l (a b) d c -> l (b d) a c", b=2)
            uvv = dsa_w_uv.rearrange("l h c d -> l c h d")
            upv = ffn_w_up.rearrange("l (k p) (g j n) -> l g j p k n", p=P, g=2, n=2 * P)
            dnv = ffn_w_down.rearrange("l (j k p) n -> l j p k n", p=P, k=2)
            with sp.Fori(0, DEPTH) as l:
                W = win[l]
                for u, c in ((U_CQ, C_CQ), (U_KV, C_KV), (U_HF, C_HF), (U_HF + 1, C_HF + 256), (U_HQ, C_HQ), (U_HQ + 1, C_HQ + 256)):
                    if u == 3:
                        sp.wait_ge(low_head, nth(low_head, l, 1))
                        sp.sem_inc(slot_seen, 1)
                    load_unit(sp, l, u, W[:, :, c:c + 256])
                    if u == U_HF:
                        sp.dma_start(w_uk[:, :, :], ukv[l]).then_inc(small_in, 16)
                        sp.dma_start(w_uv[:, :, :], uvv[l]).then_inc(small_in, 16)
                load_unit(sp, l, U_UQ, uqv[l])
                load_unit(sp, l, U_RQ, W[:, :, C_RQ:C_RQ + 256])
                load_unit(sp, l, U_RK, W[:, :, C_RK:C_RK + 256])
                for u, c in ((U_HV, C_HV), (U_RV, C_RV), (U_RG, C_RG), (U_HGATE, C_HG)):
                    for half in range(2):
                        load_unit(sp, l, u + half, W[:, 4 * half:4 * half + 4, c:c + 512])
                for g in range(12):
                    load_unit(sp, l, U_GT + g, W[:, :, C_GT + 256 * g:C_GT + 256 * (g + 1)])
                for nb in range(2):
                    for b in range(3):
                        load_unit(sp, l, U_BR + 3 * nb + b, brv[b][l][:, :, 512 * nb:512 * nb + 512])
                for i in range(4):
                    load_unit(sp, l, U_WO + i, wov[l][:, 2 * i:2 * i + 2, :])
                up_l, dn_l = upv[l], dnv[l]
                load_unit(sp, l, U_FF, up_l[0, 0])
                load_unit(sp, l, U_FF + 1, up_l[1, 0])
                load_unit(sp, l, U_FF + 2, up_l[0, 1])
                load_unit(sp, l, U_FF + 3, up_l[1, 1])
                load_unit(sp, l, U_FF + 4, dn_l[0])
                with sp.Fori(0, NPAIR - 2) as j:
                    load_unit(sp, l, U_FF + 5, up_l[0, j + 2], step=j)
                    load_unit(sp, l, U_FF + 6, up_l[1, j + 2], step=j)
                    load_unit(sp, l, U_FF + 7, dn_l[j + 1], step=j)
                load_unit(sp, l, UNITS - 1, dn_l[NPAIR - 1])
            for t in range(TT):
                sp.wait_ge(x_new, 4 * DEPTH + 2 + t + 1)
                sp.dma_start(out[0, t * P:(t + 1) * P, :], xr[:, t, :]).then_inc(y_out, 16)
            sp.wait_ge(y_out, 16 * TT)

        @block.tensor
        def _(pe):
            mm = nc.tensor.matmul

            def three(o, a_up, a_low, b_up, b_low, first, last):
                mm(o, a_up, b_up, start=first, stop=False)
                mm(o, a_up, b_low, start=False, stop=False)
                return mm(o, a_low, b_up, start=False, stop=last)

            def columns_out(s, w, c, n_k, o, a_up, a_low, wait_k=None):
                for k in range(n_k):
                    if wait_k:
                        wait_k(k)
                    wu = up[s][:, :].rearrange("p (k n) -> p k n", n=w)[:, k, c:c + P]
                    wl = low[s][:, :].rearrange("p (k n) -> p k n", n=w)[:, k, c:c + P]
                    i = three(o, wu, wl, a_up[:, k, :], a_low[:, k, :], k == 0, k == n_k - 1)
                return i

            def tokens_out(s, w, ks, k0, o_of, a_up, a_low, first, last, tiles=range(TT)):
                for k in range(ks):
                    for t in tiles:
                        for c in range(w // 512):
                            wu = up[s][:, :].rearrange("p (k n) -> p k n", n=w)[:, k, 512 * c:512 * c + 512]
                            wl = low[s][:, :].rearrange("p (k n) -> p k n", n=w)[:, k, 512 * c:512 * c + 512]
                            au = a_up[:, k0 + k, t * P:(t + 1) * P]
                            al = a_low[:, k0 + k, t * P:(t + 1) * P]
                            o = o_of(t, c)
                            mm(o, au, wu, start=first and k == 0, stop=False)
                            mm(o, au, wl, start=False, stop=False)
                            i = mm(o, al, wu, start=False, stop=last and k == ks - 1)
                return i

            def transposed_x(l, stage):
                for t in range(TT):
                    pe.wait_ge(xs_ready, nth(xs_ready, l, 2 * stage + t + 1))
                    for k in range(KD):
                        i = nc.tensor.transpose(ps[:, 4 + k // 2, (k % 2) * T + t * P:(k % 2) * T + (t + 1) * P],
                                                xs[:, t, k * P:(k + 1) * P], ident)
                        if t == 1 and k % 2:
                            i.then_inc(xT_ready, 1)

            pe.wait_ge(setup_in, 16 * 3)
            mm(ps[0:HD, 0, 0:384], relb[0:32, :], onehot[0:32, :], start=True, stop=True).then_inc(setup_ps, 1)

            with pe.Fori(0, DEPTH) as l:
                transposed_x(l, 0)

                def x_part(k):
                    pe.wait_ge(h_low_done, nth(h_low_done, l, k + 1))

                pe.wait_ge(low_head, nth(low_head, l, 1))
                pe.wait_ge(low_done[U_CQ % SLOTS], fill(l, U_CQ))
                columns_out(0, 256, 0, KD, ps[:, 0, 0:T], h_up, h_low, x_part)
                columns_out(0, 256, P, KD, ps[:, 0, T:2 * T], h_up, h_low).then_inc(unit_used, 1)
                pe.wait_ge(low_done[U_KV % SLOTS], fill(l, U_KV))
                columns_out(1, 256, 0, KD, ps[:, 1, 0:T], h_up, h_low)
                columns_out(1, 256, P, KD, ps[:, 1, T:2 * T], h_up, h_low).then_inc(unit_used, 1)

                def transposed_unit(u, b):
                    pe.wait_ge(low_done[u % SLOTS], fill(l, u))
                    columns_out(u % SLOTS, 256, 0, KD, ps[:, b, 0:T], h_up, h_low)
                    columns_out(u % SLOTS, 256, P, KD, ps[:, b, T:2 * T], h_up, h_low).then_inc(unit_used, 1)

                def token_units(u, b, half):
                    pe.wait_ge(low_done[(u + half) % SLOTS], fill(l, u + half))
                    tokens_out((u + half) % SLOTS, 512, 4, 4 * half, lambda t, c: ps[:, b + t, :], h_up, h_low,
                               half == 0, half == 1).then_inc(unit_used, 1)

                def index_weights():
                    for t in range(TT):
                        i = nc.tensor.transpose(ps[:, 5, HD * t:HD * (t + 1)], iwT[64:64 + HD, t * P:(t + 1) * P],
                                                kc[64:64 + HD, K_ID + 64:K_ID + 64 + HD])
                    i.then_inc(wi_ps, 1)

                def sums_of_squares():
                    pe.wait_ge(sq_ready, nth(sq_ready, l, 1))
                    for t in range(TT):
                        c = slice(t * P, (t + 1) * P)
                        mm(ps[:, 7, 32 + t:33 + t], sq[:, 0, c], ones[:, 0:1], start=True, stop=False)
                        mm(ps[:, 7, 32 + t:33 + t], sq[:, 1, c], ones[:, 0:1], start=False, stop=True)
                    for t in range(TT):
                        i = mm(ps[:, 7, 34 + t:35 + t], sq[:, 2, t * P:(t + 1) * P], ones[:, 0:1], start=True, stop=True)
                    i.then_inc(ss_ready, 1)

                def spread_rstd():
                    pe.wait_ge(diag_ready, nth(diag_ready, l, 1))
                    mm(ps[:, 6, :], ones, diag[:, :, :].rearrange("p a b -> p (a b)"), start=True, stop=True).then_inc(bc_ready, 1)

                def latent_values():
                    pe.wait_ge(c_ready, nth(c_ready, l, 1))
                    pe.wait_ge(small_in, nth(small_in, l, 32))
                    for t in range(TT):
                        i = mm(ps[:, 4 + t, :], ckvT[:, t * P:(t + 1) * P], w_uv[:, :, :].rearrange("p h d -> p (h d)"),
                               start=True, stop=True)
                    i.then_inc(v_ready, 1)

                def index_scores(h):
                    b, r = 64 * (h % 2), h // 2
                    if h < 2:
                        pe.wait_ge(vlat_ready, nth(vlat_ready, l, 1))
                        pe.wait_ge(ik_twice, nth(ik_twice, l, 16))
                    if h >= 4:
                        pe.wait_ge(relu_done, nth(relu_done, l, h - 3))
                    o = ps[:, 4 + h % 4, :]
                    mm(o[:, 0:P], qiT[b:b + 64, r, 0:P], ikT[b:b + 64, 0:P], start=True, stop=True)
                    mm(o[:, P:3 * P], qiT[b:b + 64, r, P:T], ikT[b:b + 64, :], start=True, stop=True).then_inc(idx_ready, 1)

                def rotate():
                    pe.wait_ge(evac, nth(evac, l, 6))
                    pe.wait_ge(relu_done, nth(relu_done, l, HD))
                    for i4 in range(4):
                        i = mm(ps[:, 4 + i4 // 2, (i4 % 2) * T:(i4 % 2 + 1) * T], rot, qk[:, i4, :], start=True, stop=True)
                    i.then_inc(rot_ready, 1)

                def retention_dots(h):
                    b, r = 64 * (h % 2), h // 2
                    if h == 0:
                        pe.wait_ge(qkr_ready, nth(qkr_ready, l, 1))
                    if h >= 2:
                        pe.wait_ge(dec_ready, nth(dec_ready, l, h - 1))
                    o = ps[:, 4 + h % 2, :]
                    mm(o[:, 0:T], qkr[b:b + 64, 2 + r, 0:P], qkr[b:b + 64, r, :], start=True, stop=True)
                    mm(o[:, T:T + P], qkr[b:b + 64, 2 + r, P:T], qkr[b:b + 64, r, P:T], start=True, stop=True).then_inc(dot_ready, 1)

                def weighted_values(b, first, cross, second, v):
                    for h in range(4):
                        c = slice(h * P, (h + 1) * P)
                        mm(ps[:, b, c], first(h), v[:, 0, c], start=True, stop=True)
                        mm(ps[:, b + 1, c], cross(h), v[:, 0, c], start=True, stop=False)
                        i = mm(ps[:, b + 1, c], second(h), v[:, 1, c], start=False, stop=True)
                    return i

                def retention_out():
                    pe.wait_ge(dec_ready, nth(dec_ready, l, HR))
                    pe.wait_ge(evac, nth(evac, l, 8))
                    weighted_values(4, lambda h: dec[:, h, 0:P], lambda h: dec[:, h, P:T], lambda h: dec[:, h, T:T + P], v_r) \
                        .then_inc(oret_ready, 1)

                def hgrn_level(v):
                    if v == -1:
                        pe.wait_ge(fk_ready, nth(fk_ready, l, 1))
                        pe.wait_ge(evac, nth(evac, l, 3))
                        pe.wait_ge(relu_done, nth(relu_done, l, HD))
                        for a in range(8):
                            c = slice((a % 4) * T + (a // 4) * P, (a % 4) * T + (a // 4) * P + P)
                            i = mm(ps[:, 6 + a // 4, (a % 4) * P:(a % 4 + 1) * P], hgk[:, c], hgq[:, c], start=True, stop=True)
                    else:
                        pe.wait_ge(lvl_next, nth(lvl_next, l, v + 1))
                        if v == 0:
                            pe.wait_ge(lvl_used, nth(lvl_used, l, 1))
                        elif v >= 2:
                            pe.wait_ge(lvl_used, nth(lvl_used, l, v))
                        m = 1 << v
                        b = 6 + v % 2
                        if v < LEVELS:
                            for a in range(8):
                                c = slice((a % 4) * T + (a // 4) * P, (a % 4) * T + (a // 4) * P + P)
                                later = hgq[:, c].rearrange("p (b two m) -> p b two m", two=2, m=m)[:, :, 1, :]
                                i = mm(ps[:, b, a * 64:(a + 1) * 64], hgk[:, c], later, start=True, stop=True)
                        else:
                            for h in range(HG):
                                i = mm(ps[:, b, h * P:(h + 1) * P], hgk[:, h * T:h * T + P], hgq[:, h * T + P:(h + 1) * T], start=True, stop=True)
                    i.then_inc(lvl_ready, 1)

                def hgrn_out():
                    pe.wait_ge(lvl_used, nth(lvl_used, l, 9))
                    pe.wait_ge(evac, nth(evac, l, 7))
                    weighted_values(6, lambda h: att[:, h, :], lambda h: att2[:, h, :], lambda h: att[:, 4 + h, :], v_h) \
                        .then_inc(ohg_ready, 1)

                def transposed_y(b, y, ready, done):
                    pe.wait_ge(ready, nth(ready, l, 1))
                    if b == 4:
                        pe.wait_ge(qlat_ready, nth(qlat_ready, l, 2))
                    for k in range(4):
                        for t in range(TT):
                            i = nc.tensor.transpose(ps[:, b + k // 2, (k % 2) * T + t * P:(k % 2) * T + (t + 1) * P],
                                                    y[:, t, k * P:(k + 1) * P], ident)
                    i.then_inc(done, 1)

                def latent_queries(r):
                    pe.wait_ge(ynr_ready, nth(ynr_ready, l, 1))
                    if r:
                        pe.wait_ge(qlat_ready, nth(qlat_ready, l, 1))
                    for h in range(4 * r, 4 * r + 4):
                        b = 64 * (h % 2)
                        i = mm(ps[:, 4 + h % 2, (h // 2 % 2) * T:(h // 2 % 2 + 1) * T], w_uk[b:b + 64, h // 2, :], qT[b:b + 64, h // 2, :],
                               start=True, stop=True)
                    i.then_inc(qlat_ps, 1)

                def attention_step(h):
                    if h < HD:
                        if h == 0:
                            pe.wait_ge(qlat_ready, nth(qlat_ready, l, 2))
                            pe.wait_ge(yret_done, nth(yret_done, l, 1))
                        if h >= 2:
                            pe.wait_ge(pT_ready, nth(pT_ready, l, h - 1))
                        o = ps[:, 4 + h % 2, :]
                        mm(o[:, 0:P], qlat[:, h, 0:P], ckvT[:, 0:P], start=True, stop=True)
                        mm(o[:, P:3 * P], qlat[:, h, P:T], ckvT[:, :], start=True, stop=True).then_inc(lg_ready, 1)
                    if 1 <= h <= HD:
                        g = h - 1
                        pe.wait_ge(prob_ready, nth(prob_ready, l, g + 1))
                        for c in range(3):
                            i = nc.tensor.transpose(ps[:, 4 + g % 2, c * P:(c + 1) * P], probs[:, g % 2, c * P:(c + 1) * P], ident)
                        i.then_inc(pT_ps, 1)
                    if h >= 2:
                        g = h - 2
                        pe.wait_ge(pT_ready, nth(pT_ready, l, g + 1))
                        if g == 0:
                            pe.wait_ge(yhg_done, nth(yhg_done, l, 1))
                        b, r = 64 * (g % 2), g // 2
                        o = ps[b:b + 64, 6 + r // 2, (r % 2) * T:(r % 2 + 1) * T]
                        mm(o, vlat[:, 0, g * DH:(g + 1) * DH], probsT[:, g % 2, 0:T], start=True, stop=False)
                        mm(o[:, P:T], vlat[:, 1, g * DH:(g + 1) * DH], probsT[:, g % 2, T:T + P], start=False, stop=True) \
                            .then_inc(pv_done, 1)

                transposed_unit(U_HF, 2)
                sums_of_squares()
                index_weights()
                transposed_unit(U_HF + 1, 3)
                spread_rstd()
                pe.wait_ge(evac, nth(evac, l, 1))
                transposed_unit(U_HQ, 0)
                transposed_unit(U_HQ + 1, 1)
                latent_values()
                pe.wait_ge(low_done[U_UQ % SLOTS], fill(l, U_UQ))
                pe.wait_ge(evac, nth(evac, l, 2))
                for i in range(4):
                    o = columns_out(0, 1024, 512 + i * P, 2, ps[:, 2 + i // 2, (i % 2) * T:(i % 2 + 1) * T], cq_up, cq_low)
                o.then_inc(uqi_ready, 1)
                pe.wait_ge(evac, nth(evac, l, 3))
                for i in range(4):
                    o = columns_out(0, 1024, i * P, 2, ps[:, i // 2, (i % 2) * T:(i % 2 + 1) * T], cq_up, cq_low)
                o.then_inc(unit_used, 1)
                pe.wait_ge(evac, nth(evac, l, 4))
                transposed_unit(U_RQ, 2)
                for h in range(4):
                    index_scores(h)
                transposed_unit(U_RK, 3)
                for h in range(4, HD):
                    index_scores(h)
                pe.wait_ge(evac, nth(evac, l, 5))
                token_units(U_HV, 0, 0)
                hgrn_level(-1)
                rotate()
                token_units(U_HV, 0, 1)
                hgrn_level(0)
                pe.wait_ge(evac, nth(evac, l, 6))
                token_units(U_RV, 2, 0)
                hgrn_level(1)
                retention_dots(0)
                retention_dots(1)
                token_units(U_RV, 2, 1)
                hgrn_level(2)
                retention_dots(2)
                retention_dots(3)
                pe.wait_ge(evac, nth(evac, l, 7))
                token_units(U_RG, 0, 0)
                hgrn_level(3)
                retention_out()
                token_units(U_RG, 0, 1)
                hgrn_level(4)
                pe.wait_ge(evac, nth(evac, l, 8))
                token_units(U_HGATE, 2, 0)
                hgrn_level(5)
                token_units(U_HGATE, 2, 1)
                hgrn_level(6)
                for g in range(12):
                    u, b = U_GT + g, [0, 1, 2, 3][g % 4]
                    if g == 0:
                        pe.wait_ge(silur_ready, nth(silur_ready, l, 1))
                    elif g == 2:
                        pe.wait_ge(siluh_ready, nth(siluh_ready, l, 1))
                    elif g % 2 == 0:
                        pe.wait_ge(evac, nth(evac, l, 8 + g // 2 - 1))
                    transposed_unit(u, b)
                    if g == 0:
                        hgrn_level(7)
                        latent_queries(0)
                    if g == 1:
                        hgrn_out()
                        latent_queries(1)
                    if g == 2:
                        transposed_y(4, yn_r, ynr_ready, yretT)
                    if g == 3:
                        transposed_y(6, yn_h, ynh_ready, yhgT)
                    if g >= 3:
                        attention_step(g - 3)
                for nb in range(2):
                    for b in range(3):
                        j = 3 * nb + b
                        u = U_BR + j
                        pe.wait_ge(low_done[u % SLOTS], fill(l, u))
                        if j < 2:
                            pe.wait_ge(evac, nth(evac, l, 13 + j))
                        else:
                            pe.wait_ge(br_used, nth(br_used, l, j - 1))
                        if b == 2 and nb == 0:
                            pe.wait_ge(ydsa_done, nth(ydsa_done, l, 1))
                        yu, yl = ((yret_up, yret_low), (yhg_up, yhg_low), (ydsa_up, ydsa_low))[b]
                        for i in range(4):
                            o = columns_out(u % SLOTS, 512, i * P, 4, ps[:, 2 * (j % 2) + i // 2, (i % 2) * T:(i % 2 + 1) * T], yu, yl)
                        o.then_inc(unit_used, 1)
                        if j == 0:
                            attention_step(HD + 1)
                def out_rows(i, tiles, first, last):
                    return tokens_out((U_WO + i) % SLOTS, 1024, 2, 2 * i, lambda t, c: ps[:, 2 * t + c, :], h_up, h_low, first, last, tiles)

                pe.wait_ge(low_done[U_WO % SLOTS], fill(l, U_WO))
                pe.wait_ge(mrg_done, nth(mrg_done, l, 1))
                pe.wait_ge(br_used, nth(br_used, l, 5))
                out_rows(0, [0], True, False)
                pe.wait_ge(br_used, nth(br_used, l, 6))
                out_rows(0, [1], True, False).then_inc(unit_used, 1)
                pe.wait_ge(low_done[(U_WO + 1) % SLOTS], fill(l, U_WO + 1))
                out_rows(1, [0, 1], False, False).then_inc(unit_used, 1)
                pe.wait_ge(low_done[(U_WO + 2) % SLOTS], fill(l, U_WO + 2))
                pe.wait_ge(mrg_done, nth(mrg_done, l, 2))
                out_rows(2, [0], False, False)
                pe.wait_ge(low_done[(U_WO + 3) % SLOTS], fill(l, U_WO + 3))
                out_rows(3, [0], False, True).then_inc(o_ready, 1)
                out_rows(2, [1], False, False).then_inc(unit_used, 1)
                out_rows(3, [1], False, True).then_inc(unit_used, 1)

                transposed_x(l, 1)

                def ffn_up(u, b, step, wait_x=None):
                    pe.wait_ge(low_done[u % SLOTS], fill(l, u, step))
                    columns_out(u % SLOTS, 256, 0, KD, ps[:, b, 0:T], h_up, h_low, wait_x)
                    columns_out(u % SLOTS, 256, P, KD, ps[:, b, T:2 * T], h_up, h_low).then_inc(unit_used, 1)

                def ffn_down(u, j, step, first, last):
                    pe.wait_ge(low_done[u % SLOTS], fill(l, u, step))
                    pe.wait_ge(glow_done, nth(glow_done, l, j + 1))
                    if last:
                        tokens_out(u % SLOTS, 1024, 2, 0, lambda t, c: ps[:, 2 * t + c, :], *g_last, False, True, [0]) \
                            .then_inc(o_ready, 1)
                        tokens_out(u % SLOTS, 1024, 2, 0, lambda t, c: ps[:, 2 * t + c, :], *g_last, False, True, [1]) \
                            .then_inc(unit_used, 1)
                    else:
                        tokens_out(u % SLOTS, 1024, 2, 0, lambda t, c: ps[:, 2 * t + c, :], g_up, g_low, first, False) \
                            .then_inc(unit_used, 1)

                def ffn_x(k):
                    pe.wait_ge(h_low_done, nth(h_low_done, l, KD + k + 1))

                pe.wait_ge(h_low_done, nth(h_low_done, l, KD + 2))
                ffn_up(U_FF, 4, 0, ffn_x)
                ffn_up(U_FF + 1, 5, 0)
                pe.wait_ge(cva_done, nth(cva_done, l, 1))
                ffn_up(U_FF + 2, 4, 0)
                pe.wait_ge(cvu_done, nth(cvu_done, l, 1))
                ffn_up(U_FF + 3, 5, 0)
                ffn_down(U_FF + 4, 0, 0, True, False)
                with pe.Fori(0, NPAIR - 2) as j:
                    pe.wait_ge(cva_done, nth(cva_done, l, j + 2))
                    ffn_up(U_FF + 5, 4, j)
                    pe.wait_ge(cvu_done, nth(cvu_done, l, j + 2))
                    ffn_up(U_FF + 6, 5, j)
                    ffn_down(U_FF + 7, j + 1, j, False, False)
                ffn_down(UNITS - 1, NPAIR - 1, 0, False, True)

        @block.scalar
        def _(act):
            f = nc.scalar.activation
            act.dma_start(kc[:, 0:K_MAT], consts[:, 0:K_MAT]).then_inc(setup_in, 16)
            act.dma_start(prm_all[:, :, :], params).then_inc(prm_in, 16)
            act.wait_ge(x_in[0], 16)
            f(junk[:, :], xr[:, 0, :], ACT.Square, accum_out=ss[:, 0:1]).then_inc(x_sq, 1)
            act.wait_ge(setup_ps, 1)
            f(brow[0:HD, :], ps[0:HD, 0, 0:384], ACT.Copy).then_inc(setup_cp, 1)
            act.wait_ge(setup_done, 1)
            for i in range(DEPTH):
                o = f(lbs[:, i, 2, :], lbs[:, i, 3, :], ACT.Exp)
            o.then_inc(setup_v, 1)

            with act.Fori(0, DEPTH) as l:
                def x_squares(stage, t):
                    act.drain()
                    if stage == 0:
                        act.wait_ge(x_in[t], 16)
                    act.wait_ge(x_new, nth(x_new, l, 2 + 2 * stage + t + 1))
                    f(junk[:, :], xr[:, t, :], ACT.Square, accum_out=ss[:, t:t + 1]).then_inc(x_sq, 1)

                def x_stage(stage, g0):
                    x_squares(stage, 1)
                    split_up(act, l, 40 if stage else 0)
                    if stage == 0:
                        act.wait_ge(prm_ready, nth(prm_ready, l, 1))
                    for k in range(KD):
                        if k % 2 == 0:
                            act.wait_ge(xT_ready, nth(xT_ready, l, 4 * stage + k // 2 + 1))
                        o = f(h_up[:, k, :], ps[:, 4 + k // 2, (k % 2) * T:(k % 2 + 1) * T], ACT.Copy, scale=prm[:, g0 + k:g0 + k + 1])
                        if k % 2:
                            o.then_inc(h_up_done, 1)

                def o_stage(stage, units):
                    act.wait_ge(o_ready, nth(o_ready, l, stage + 1))
                    for t in range(TT):
                        if t == 1:
                            act.wait_ge(unit_used, used(l, units))
                        f(junk[:, 0:512], ps[:, 2 * t, :], ACT.Square, accum_out=oss[:, t:t + 1]).then_inc(o_sq_half, 1)
                        if t == 1 and stage == 0:
                            x_squares(1, 0)
                            act.drain()
                        act.wait_ge(og_half, nth(og_half, l, 2 * stage + t + 1))
                        f(junk[:, 512:D], ps[:, 2 * t + 1, :], ACT.Square, accum_out=oss[:, 2 + t:3 + t]).then_inc(o_sq, 1)
                        act.drain()
                    if stage == 1:
                        x_squares(2, 0)

                x_stage(0, Q_PRE)
                split_up(act, l, 1)
                split_up(act, l, 2)
                act.wait_ge(unit_used, used(l, 1))
                f(sq[:, 0:2, :].rearrange("p a b -> p (a b)"), ps[:, 0, :], ACT.Square)
                for i in range(2):
                    f(zs[:, i, :], ps[:, 0, i * T:(i + 1) * T], ACT.Copy, scale=prm[:, Q_QN + i:Q_QN + i + 1])
                split_up(act, l, 3)
                act.wait_ge(unit_used, used(l, 2))
                f(iwT[64:64 + HD, :], ps[64:64 + HD, 1, T:2 * T], ACT.Copy)
                f(sq[:, 2, :], ps[:, 1, 0:T], ACT.Square).then_inc(sq_ready, 1)
                f(zs[:, 2, :], ps[:, 1, 0:T], ACT.Copy, scale=prm[:, Q_KVN:Q_KVN + 1]).then_inc(zs_ready, 1)
                f(ikT[0:64, :], ps[0:64, 1, T:2 * T], ACT.Copy).then_inc(evac, 1)
                act.wait_ge(evac, nth(evac, l, 1))
                act.dma_start(ikT[64:128, :], ikT[0:64, :]).then_inc(ik_twice, 16)
                split_up(act, l, 4)
                split_up(act, l, 5)
                act.wait_ge(unit_used, used(l, 4))
                f(hgf[:, :], wide(2), ACT.Sigmoid)
                f(hgk[:, :], wide(2), ACT.Sigmoid, scale=-1.0).then_inc(evac, 1)
                split_up(act, l, 6)
                split_up(act, l, 7)
                act.wait_ge(unit_used, used(l, 6))
                f(hgq[:, :], wide(0), ACT.Copy).then_inc(evac, 1)
                act.wait_ge(v_ready, nth(v_ready, l, 1))
                f(vlat[:, :, :].rearrange("p a b -> p (a b)"), wide(4), ACT.Copy).then_inc(vlat_ready, 1)
                split_up(act, l, 8)
                act.wait_ge(uqi_ready, nth(uqi_ready, l, 1))
                f(qiT[:, :, :].rearrange("p a b -> p (a b)"), wide(2), ACT.Copy).then_inc(evac, 1)
                act.wait_ge(unit_used, used(l, 7))
                act.wait_ge(bias_out, 16)
                f(qT[:, :, :].rearrange("p a b -> p (a b)"), wide(0), ACT.Copy).then_inc(evac, 1)
                split_up(act, l, 9)

                def relus(hs):
                    for h in hs:
                        act.wait_ge(idx_ready, nth(idx_ready, l, h + 1))
                        if h >= 2:
                            act.wait_ge(relu_used, nth(relu_used, l, h - 1))
                        f(probs[:, h % 2, :], ps[:, 4 + h % 4, 0:384], ACT.Relu).then_inc(relu_done, 1)

                relus(range(0, 4))
                split_up(act, l, 10)
                act.wait_ge(unit_used, used(l, 9))
                f(qk[:, :, :].rearrange("p a b -> p (a b)"), wide(2), ACT.Copy).then_inc(evac, 1)
                relus(range(4, 8))
                split_up(act, l, 11)
                split_up(act, l, 12)
                act.wait_ge(unit_used, used(l, 11))
                f(v_h[:, :, :].rearrange("p a b -> p (a b)"), wide(0), ACT.Copy).then_inc(evac, 1)
                split_up(act, l, 13)
                split_up(act, l, 14)
                act.wait_ge(unit_used, used(l, 13))
                f(v_r[:, :, :].rearrange("p a b -> p (a b)"), wide(2), ACT.Copy).then_inc(evac, 1)
                split_up(act, l, 15)
                split_up(act, l, 16)
                act.wait_ge(unit_used, used(l, 15))
                f(silu_r[:, :, :].rearrange("p a b -> p (a b)"), wide(0), ACT.Sigmoid).then_inc(sgr_ready, 1)
                split_up(act, l, 17)
                split_up(act, l, 18)
                act.wait_ge(unit_used, used(l, 17))
                f(silu_h[:, :, :].rearrange("p a b -> p (a b)"), wide(2), ACT.Sigmoid).then_inc(sgh_ready, 1)

                def gate_job(j):
                    act.wait_ge(unit_used, used(l, U_GT + 2 * j + 2))
                    if j < 3:
                        act.wait_ge(lvl_used, nth(lvl_used, l, 9))
                        act.wait_ge(qkr_ready, nth(qkr_ready, l, 1))
                    f(gates[:, 4 * j:4 * j + 4, :].rearrange("p a b -> p (a b)"), wide(2 * (j % 2)), ACT.Tanh, scale=0.5) \
                        .then_inc(evac, 1)

                def queries_out(r):
                    act.wait_ge(qlat_ps, nth(qlat_ps, l, r + 1))
                    for b in range(2):
                        o = f(qlat[:, 4 * r + b:4 * r + 4:2, :], ps[:, 4 + b, :].rearrange("p (a b) -> p a b", a=2), ACT.Copy, scale=DH ** -0.5)
                    o.then_inc(qlat_ready, 1)

                def exps(h):
                    act.wait_ge(nmax_ready, nth(nmax_ready, l, h + 1))
                    b = h % 2
                    f(probs[:, b, 0:P], probs[:, b, 0:P], ACT.Exp, bias=nmax[:, 2 * b:2 * b + 1], accum_out=rsum[:, 2 * b:2 * b + 1])
                    f(probs[:, b, P:384], probs[:, b, P:384], ACT.Exp, bias=nmax[:, 2 * b + 1:2 * b + 2], accum_out=rsum[:, 2 * b + 1:2 * b + 2]) \
                        .then_inc(exp_done, 1)

                def probs_out(h):
                    act.wait_ge(pT_ps, nth(pT_ps, l, h + 1))
                    if h >= 2:
                        act.wait_ge(pv_done, nth(pv_done, l, h - 1))
                    f(probsT[:, h % 2, :], ps[:, 4 + h % 2, 0:384], ACT.Copy).then_inc(pT_ready, 1)

                split_up(act, l, 19)
                queries_out(0)
                split_up(act, l, 20)
                act.wait_ge(ohg_ready, nth(ohg_ready, l, 1))
                for t in range(TT):
                    o = f(junk[:, 512 * t:512 * (t + 1)], ps[:, 6 + t, :], ACT.Square, accum_out=hss[:, t:t + 1])
                o.then_inc(ohg_sq, 1)
                queries_out(1)
                gate_job(0)
                for g in range(2, 12):
                    split_up(act, l, U_GT + g + 2)
                    if g == 2:
                        act.wait_ge(yretT, nth(yretT, l, 1))
                        f(yret_up[:, :, :].rearrange("p a b -> p (a b)"), wide(4), ACT.Copy).then_inc(yret_upd, 1)
                    if g == 3:
                        gate_job(1)
                        act.wait_ge(yhgT, nth(yhgT, l, 1))
                        for k in range(4):
                            o = f(yhg_up[:, k, :], ps[:, 6 + k // 2, (k % 2) * T:(k % 2 + 1) * T], ACT.Copy, scale=prm[:, Q_HGN + k:Q_HGN + k + 1])
                        o.then_inc(yhg_upd, 1)
                    if g >= 3:
                        if g >= 4:
                            probs_out(g - 4)
                        if g - 3 < HD:
                            exps(g - 3)
                    if g > 3 and g % 2 == 1:
                        gate_job(g // 2)
                split_up(act, l, 31)
                act.wait_ge(pv_done, nth(pv_done, l, HD))
                f(ydsa_up[:, :, :].rearrange("p a b -> p (a b)"), wide(6), ACT.Copy).then_inc(ydsa_upd, 1)
                act.dma_start(gpost[:, :], ln_mix_post[l].partition_broadcast(P)).then_inc(gpost_in, 16)
                for u in range(32, 36):
                    split_up(act, l, u)
                    if u == 33:
                        act.wait_ge(mrg_ready, nth(mrg_ready, l, 1))
                        f(h_up[:, 0:4, :].rearrange("p a b -> p (a b)"), mrg[:, :, :].rearrange("p a b -> p (a b)"), ACT.Copy, scale=0.5) \
                            .then_inc(mrg_up, 1)
                split_up(act, l, 36)
                act.wait_ge(mrg_ready, nth(mrg_ready, l, 2))
                f(h_up[:, 4:8, :].rearrange("p a b -> p (a b)"), mrg[:, :, :].rearrange("p a b -> p (a b)"), ACT.Copy, scale=0.5) \
                    .then_inc(mrg_up, 1)
                for u in range(37, 40):
                    split_up(act, l, u)
                o_stage(0, U_FF)
                x_stage(1, Q_FFN)
                act.dma_start(gpost[:, :], ln_ffn_post[l].partition_broadcast(P)).then_inc(gpost_in, 16)

                def conv(half, j, n_units, step, c, ready, base_sig):
                    act.drain()
                    act.wait_ge(unit_used, used(l, n_units, step))
                    act.wait_ge(cvp_ready, nth(cvp_ready, l, j + 1))
                    for i in range(2):
                        o = f(c[:, i, :], ps[:, 4 + half, i * T:(i + 1) * T], ACT.Identity,
                              bias=cvp[:, 0, half, i:i + 1], scale=cvp[:, 3, half, i:i + 1])
                    o.then_inc(base_sig, 1)

                def gelu(j):
                    act.wait_ge(cva_done, nth(cva_done, l, j + 1))
                    f(gel[:, :, :], cva[:, :, :], ACT.Gelu_apprx_tanh).then_inc(gel_done, 1)

                def g_upper(j, dst):
                    act.wait_ge(gf_done, nth(gf_done, l, j + 1))
                    f(dst[:, :, :], gf[:, :, :], ACT.Copy).then_inc(gup_done, 1)

                split_up(act, l, 41)
                conv(0, 0, U_FF + 1, 0, cva, None, cva_base)
                split_up(act, l, 42)
                conv(1, 0, U_FF + 2, 0, cvu, None, cvu_base)
                gelu(0)
                g_upper(0, g_up)
                split_up(act, l, 43)
                with act.Fori(0, NPAIR - 2) as j:
                    split_up(act, l, 44, step=j)
                    conv(0, j + 1, U_FF + 3, j, cva, None, cva_base)
                    split_up(act, l, 45, step=j)
                    conv(1, j + 1, U_FF + 4, j, cvu, None, cvu_base)
                    gelu(j + 1)
                    split_up(act, l, 46, step=j)
                    act.wait_ge(unit_used, used(l, U_FF + 5, j))
                    g_upper(j + 1, g_up)
                split_up(act, l, UNITS - 1)
                conv(0, NPAIR - 1, UNITS - 3, 0, cva, None, cva_base)
                conv(1, NPAIR - 1, UNITS - 2, 0, cvu, None, cvu_base)
                gelu(NPAIR - 1)
                g_upper(NPAIR - 1, g_last[0])
                f(small[:, 176:177], nhalf[:, 0:1], ACT.Exp)
                o_stage(1, UNITS)

        @block.vector
        def _(dve):
            v = nc.vector

            def settle():
                dve.drain()

            lb4, rec4, cum4 = small[:, 84:88], small[:, 88:92], small[:, 92:96]
            v.memset(nhalf, -0.5)
            dve.wait_ge(prm_in, 16)
            v.tensor_copy(lb4, prm_all[:, 0, Q_LB:Q_LB + 4])
            settle()
            for i in range(1, DEPTH):
                v.tensor_tensor(lb4, lb4, prm_all[:, i, Q_LB:Q_LB + 4], ALU.max)
                settle()
            for i in range(DEPTH):
                o = v.tensor_tensor(lbs[:, i, 3, :], prm_all[:, i, Q_LB:Q_LB + 4], lb4, ALU.subtract)
            o.then_inc(setup_done, 1)
            dve.wait_ge(x_sq, 1)
            v.tensor_scalar(ss[:, 0:1], ss[:, 0:1], 1.0 / D, EPS, ALU.mult, ALU.add).then_inc(n_var, 1)
            dve.wait_ge(setup_v, 1)
            v.tensor_copy(cum4, lbs[:, 0, 2, :])
            settle()
            for i in range(1, DEPTH):
                v.tensor_tensor(cum4, cum4, lbs[:, i, 2, :], ALU.add)
                settle()
            v.reciprocal(rec4, cum4)
            settle()
            for i in range(DEPTH):
                v.tensor_tensor(lbs[:, i, 2, :], lbs[:, i, 2, :], rec4, ALU.mult)
            settle()
            v.tensor_copy(cum4, lbs[:, 0, 2, :])
            settle()
            for i in range(DEPTH):
                if i:
                    v.tensor_tensor(cum4, cum4, lbs[:, i, 2, :], ALU.add)
                    settle()
                v.tensor_tensor(lbs[:, i, 0, :], cum4, lbs[:, 0, 2, :], ALU.subtract)
                settle()
                v.tensor_scalar(lbs[:, i, 0, :], lbs[:, i, 0, :], 0.0, 1.0, ALU.max, ALU.min)
                settle()
                v.tensor_scalar(lbs[:, i, 1, :], lbs[:, i, 0, :], -1.0, 1.0, ALU.mult, ALU.add)

            dve.wait_ge(n_rs, 1)
            v.tensor_scalar(xs[:, 0, :], xr[:, 0, :], rs[:, 0:1], None, ALU.mult).then_inc(xs_ready, 1)

            with dve.Fori(0, DEPTH) as l:
                settle()
                v.tensor_copy(lbc, lbs[:, l, 0:2, :].rearrange("p a b -> p (a b)"))
                v.tensor_copy(prm[:, :], prm_all[:, l, :]).then_inc(prm_ready, 1)

                def lower(u, step=0):
                    split_low(nc.vector, l, u, step)

                def x_var(stage, t):
                    dve.wait_ge(x_sq, nth(x_sq, l, 2 * stage + t + 1))
                    v.tensor_scalar(ss[:, t:t + 1], ss[:, t:t + 1], 1.0 / D, EPS, ALU.mult, ALU.add).then_inc(n_var, 1)

                def x_scaled(stage, t):
                    dve.wait_ge(n_rs, nth(n_rs, l, 2 * stage + t + 1))
                    v.tensor_scalar(xs[:, t, :], xr[:, t, :], rs[:, t:t + 1], None, ALU.mult).then_inc(xs_ready, 1)

                def x_stage(stage, g0):
                    x_var(stage, 1)
                    x_scaled(stage, 1)
                    if stage == 0:
                        lower_share(l, 0, v, low_head)
                    for k in range(KD):
                        if k % 2 == 0:
                            dve.wait_ge(h_up_done, nth(h_up_done, l, 4 * stage + k // 2 + 1))
                        v.scalar_tensor_tensor(out=h_low[:, k, :], in0=ps[:, 4 + k // 2, (k % 2) * T:(k % 2 + 1) * T],
                                               scalar=prm[:, g0 + k:g0 + k + 1], in1=h_up[:, k, :].bitcast(F32),
                                               op0=ALU.mult, op1=ALU.subtract).then_inc(h_low_done, 1)

                def o_stage(stage):
                    dve.wait_ge(gpost_in, nth(gpost_in, l, 16 * (stage + 1)))
                    for t in range(TT):
                        if t == 0:
                            dve.wait_ge(o_ready, nth(o_ready, l, stage + 1))
                        else:
                            dve.wait_ge(unit_used, used(l, U_FF if stage == 0 else UNITS))
                        v.scalar_tensor_tensor(out=og[:, t, 512:D], in0=ps[:, 2 * t + 1, :], scalar=D ** 0.5, in1=gpost[:, 512:D],
                                               op0=ALU.mult, op1=ALU.mult).then_inc(og_half, 1)
                        dve.wait_ge(o_sq_half, nth(o_sq_half, l, 2 * stage + t + 1))
                        v.scalar_tensor_tensor(out=og[:, t, 0:512], in0=ps[:, 2 * t, :], scalar=D ** 0.5, in1=gpost[:, 0:512],
                                               op0=ALU.mult, op1=ALU.mult)
                        if t == 1 and stage == 0:
                            x_var(1, 0)
                        dve.wait_ge(o_sq, nth(o_sq, l, 2 * stage + t + 1))
                        v.scalar_tensor_tensor(out=oss[:, t:t + 1], in0=oss[:, t:t + 1], scalar=D * EPS, in1=oss[:, 2 + t:3 + t],
                                               op0=ALU.add, op1=ALU.add).then_inc(o_var, 1)
                        if t == 1 and stage == 0:
                            x_scaled(1, 0)
                        dve.wait_ge(o_rs, nth(o_rs, l, 2 * stage + t + 1))
                        v.scalar_tensor_tensor(out=xr[:, t, :], in0=og[:, t, :], scalar=ors[:, t:t + 1], in1=xr[:, t, :],
                                               op0=ALU.mult, op1=ALU.add).then_inc(x_new, 1)
                    if stage == 1:
                        x_var(2, 0)
                        x_scaled(2, 0)

                x_stage(0, Q_PRE)
                lower(1)
                dve.wait_ge(wi_ps, nth(wi_ps, l, 1))
                v.tensor_scalar(wi, ps[:, 5, 0:2 * HD], 512 ** -0.5, None, ALU.mult)
                dve.wait_ge(ss_ready, nth(ss_ready, l, 1))
                v.tensor_scalar(cs4[:, 0:2], ps[:, 7, 32:34], 1.0 / QR, EPS, ALU.mult, ALU.add)
                v.tensor_scalar(cs4[:, 2:4], ps[:, 7, 34:36], 1.0 / KVR, EPS, ALU.mult, ALU.add).then_inc(cvar, 1)
                dve.wait_ge(crs, nth(crs, l, 1))
                for i in range(4):
                    o = v.tensor_scalar(diag[:, i, :], ident, cr4[:, i:i + 1], None, ALU.mult)
                o.then_inc(diag_ready, 1)
                lower(5)
                dve.wait_ge(zs_ready, nth(zs_ready, l, 1))
                dve.wait_ge(bc_ready, nth(bc_ready, l, 1))
                v.tensor_tensor(cqT[:, :, :], zs[:, 0:2, :], ps[:, 6, 0:T].unsqueeze(1).to_broadcast([P, 2, T]), ALU.mult)
                v.tensor_tensor(ckvT[:, :], zs[:, 2, :], ps[:, 6, T:2 * T], ALU.mult)
                settle()
                v.tensor_copy(cq_up[:, :, :], cqT[:, :, :])
                settle()
                v.tensor_tensor(cq_low[:, :, :], cqT[:, :, :], cq_up[:, :, :].bitcast(F32), ALU.subtract).then_inc(c_ready, 1)
                dve.wait_ge(evac, nth(evac, l, 2))
                for h in range(HG):
                    c = slice(h * T, (h + 1) * T)
                    v.tensor_scalar(hgf[:, c], hgf[:, c], lbc[:, 4 + h:5 + h], lbc[:, h:h + 1], ALU.mult, ALU.add)
                    v.tensor_scalar(hgk[:, c], hgk[:, c], lbc[:, 4 + h:5 + h], None, ALU.mult)
                settle()
                v.tensor_scalar(hgf[:, :], hgf[:, :], FLOOR, None, ALU.max).then_inc(fk_ready, 1)
                lower(8)
                for h in range(HD):
                    dve.wait_ge(relu_done, nth(relu_done, l, h + 1))
                    for t, c in ((0, slice(0, P)), (1, slice(P, 384))):
                        w = wi[:, 8 * t + h:8 * t + h + 1]
                        if h == 0:
                            o = v.tensor_scalar(score[:, c], probs[:, 0, c], w, 0.0, ALU.mult, ALU.add)
                        else:
                            o = v.scalar_tensor_tensor(out=score[:, c], in0=probs[:, h % 2, c], scalar=w, in1=score[:, c],
                                                       op0=ALU.mult, op1=ALU.add)
                    o.then_inc(relu_used, 1)
                    settle()
                dve.wait_ge(masks_in, 16)
                v.tensor_tensor(score[:, :], score[:, :], cmask, ALU.add)
                settle()
                lower(11)

                def top_round():
                    for t, c in ((0, slice(0, P)), (1, slice(P, 384))):
                        v.max(best8[:, 8 * t:8 * t + 8], score[:, c])
                    settle()
                    for t, c in ((0, slice(0, P)), (1, slice(P, 384))):
                        v.match_replace(score[:, c], best8[:, 8 * t:8 * t + 8], score[:, c], TAKEN)
                    settle()

                def hgrn_step(n):
                    settle()
                    dve.wait_ge(lvl_ready, nth(lvl_ready, l, n + 2))
                    if n == -1:
                        v.tensor_tensor(hgq[:, :], hgq[:, :], hgf[:, :], ALU.mult).then_inc(lvl_next, 1)
                        v.tensor_tensor(att[:, :, :], ps[:, 6:8, :].rearrange("p a (b c) -> p (a b) c", c=P),
                                        ident.unsqueeze(1).to_broadcast([P, 8, P]), ALU.mult).then_inc(lvl_used, 1)
                        return
                    if n == LEVELS:
                        v.tensor_copy(att2[:, :, :].rearrange("p a b -> p (a b)"), ps[:, 6 + n % 2, :]).then_inc(lvl_used, 1)
                        return
                    m = 1 << n
                    now, nxt = (hgf, hgf2) if n % 2 == 0 else (hgf2, hgf)
                    g = now[:, 0:HG * T // m].rearrange("p (x two) -> p x two", two=2)
                    q = hgq[:, :].rearrange("p (x two m) -> p x two m", two=2, m=m)
                    k = hgk[:, :].rearrange("p (x two m) -> p x two m", two=2, m=m)
                    nx = HG * T // (2 * m)
                    v.tensor_tensor(q[:, :, 1, :], q[:, :, 1, :], g[:, :, 0:1].to_broadcast([P, nx, m]), ALU.mult)
                    v.tensor_tensor(k[:, :, 0, :], k[:, :, 0, :], g[:, :, 1:2].to_broadcast([P, nx, m]), ALU.mult).then_inc(lvl_next, 1)
                    if n < LEVELS - 1:
                        v.tensor_tensor(nxt[:, 0:nx], g[:, :, 0], g[:, :, 1], ALU.mult)
                    v.copy_predicated(
                        att[:, :, :].rearrange("p a (b two m) -> p a b two m", two=2, m=m)[:, :, :, 1, :],
                        kc[:, K_LV + 64 * n:K_LV + 64 * n + 64].bitcast(U32).rearrange("p (b m) -> p b m", m=m).unsqueeze(1)
                        .to_broadcast([P, 8, 64 // m, m]),
                        ps[:, 6 + n % 2, :].rearrange("p (a b m) -> p a b m", a=8, m=m)).then_inc(lvl_used, 1)

                dve.wait_ge(evac, nth(evac, l, 6))
                v.tensor_tensor(qkcos[:, :, :], qk[:, :, :], cos.unsqueeze(1).to_broadcast([P, 4, T]), ALU.mult)
                hgrn_step(-1)
                dve.wait_ge(rot_ready, nth(rot_ready, l, 1))
                v.tensor_tensor(qkr[:, :, :], ps[:, 4:6, :].rearrange("p a (b c) -> p (a b) c", c=T),
                                sin.unsqueeze(1).to_broadcast([P, 4, T]), ALU.mult)
                settle()
                v.tensor_tensor(qkr[:, :, :], qkr[:, :, :], qkcos[:, :, :], ALU.add).then_inc(qkr_ready, 1)

                def decay(h):
                    dve.wait_ge(dot_ready, nth(dot_ready, l, h + 1))
                    dm = kc[:, K_DM + h * T:K_DM + (h + 1) * T]
                    v.tensor_tensor(dec[:, h, 0:T], ps[:, 4 + h % 2, 0:T], dm, ALU.mult)
                    v.tensor_tensor(dec[:, h, T:T + P], ps[:, 4 + h % 2, T:T + P], dm[:, 0:P], ALU.mult).then_inc(dec_ready, 1)

                def gated(s, b, sig_in, sig_out):
                    dve.wait_ge(sig_in, nth(sig_in, l, 1))
                    sv = s[:, :, :].rearrange("p a b -> p (a b)")
                    v.tensor_tensor(sv, sv, wide(b), ALU.mult).then_inc(sig_out, 1)

                top_round()
                hgrn_step(0)
                hgrn_step(1)
                decay(0)
                decay(1)
                top_round()
                lower(14)
                hgrn_step(2)
                decay(2)
                decay(3)
                top_round()
                hgrn_step(3)
                dve.wait_ge(oret_ready, nth(oret_ready, l, 1))
                for a in range(8):
                    v.bn_stats(bn6[:, a, :], ps[:, 4 + a // 4, (a % 4) * P:(a % 4 + 1) * P])
                settle()
                for a in range(8):
                    v.bn_aggr(bna[:, a, :], bn6[:, a, :])
                settle()
                v.tensor_scalar(bnr, bna[:, :, 1], EPS, None, ALU.add).then_inc(bn_var, 1)
                top_round()
                hgrn_step(4)
                gated(silu_r, 0, sgr_ready, silur_ready)
                lower(17)
                top_round()
                hgrn_step(5)
                dve.wait_ge(bn_rs, nth(bn_rs, l, 1))
                for a in range(8):
                    v.tensor_scalar(yn_r[:, a // 4, (a % 4) * P:(a % 4 + 1) * P], ps[:, 4 + a // 4, (a % 4) * P:(a % 4 + 1) * P],
                                    bna[:, a, 0:1], bnr2[:, a:a + 1], ALU.subtract, ALU.mult)
                settle()
                v.tensor_tensor(yn_r[:, :, :], yn_r[:, :, :], silu_r[:, :, :], ALU.mult).then_inc(ynr_ready, 1)
                top_round()
                hgrn_step(6)
                top_round()
                top_round()
                v.tensor_scalar(score[:, :], score[:, :], -2e38, NEG, ALU.is_gt, ALU.mult)
                settle()
                v.tensor_tensor(score[:, :], score[:, :], cmask, ALU.min).then_inc(chosen, 1)
                hgrn_step(7)
                gated(silu_h, 2, sgh_ready, siluh_ready)
                lower(20)
                dve.wait_ge(ohg_sq, nth(ohg_sq, l, 1))
                v.tensor_scalar(hss, hss, 1.0 / 512, EPS, ALU.mult, ALU.add).then_inc(ohg_var, 1)
                dve.wait_ge(ohg_rs, nth(ohg_rs, l, 1))
                for t in range(TT):
                    o = v.scalar_tensor_tensor(out=yn_h[:, t, :], in0=ps[:, 6 + t, :], scalar=hrs[:, t:t + 1], in1=silu_h[:, t, :],
                                               op0=ALU.mult, op1=ALU.mult)
                o.then_inc(ynh_ready, 1)
                dve.wait_ge(yret_upd, nth(yret_upd, l, 1))
                v.tensor_tensor(yret_low[:, :, :].rearrange("p a b -> p (a b)"), wide(4),
                                yret_up[:, :, :].bitcast(F32).rearrange("p a b -> p (a b)"), ALU.subtract).then_inc(yret_done, 1)
                dve.wait_ge(yhg_upd, nth(yhg_upd, l, 1))
                for k in range(4):
                    o = v.scalar_tensor_tensor(out=yhg_low[:, k, :], in0=ps[:, 6 + k // 2, (k % 2) * T:(k % 2 + 1) * T],
                                               scalar=prm[:, Q_HGN + k:Q_HGN + k + 1], in1=yhg_up[:, k, :].bitcast(F32),
                                               op0=ALU.mult, op1=ALU.subtract)
                o.then_inc(yhg_done, 1)
                for h in range(HD):
                    b = h % 2
                    dve.wait_ge(lg_ready, nth(lg_ready, l, h + 1))
                    dve.wait_ge(mb_ready, nth(mb_ready, l, h + 1))
                    if h >= 2:
                        dve.wait_ge(pT_ps, nth(pT_ps, l, h - 1))
                    dve.sem_inc(lg_seen, 1)
                    for t, c in ((0, slice(0, P)), (1, slice(P, 384))):
                        v.tensor_tensor_reduce(probs[:, b, c], ps[:, 4 + b, c], mbias[:, b, c], 1.0, TAKEN, ALU.add, ALU.max,
                                               nmax[:, 2 * b + t:2 * b + t + 1])
                    settle()
                    v.tensor_scalar(nmax[:, 2 * b:2 * b + 2], nmax[:, 2 * b:2 * b + 2], -1.0, None, ALU.mult).then_inc(nmax_ready, 1)
                    if h % 3 == 1:
                        lower(23 + 3 * (h // 3))
                    dve.wait_ge(exp_done, nth(exp_done, l, h + 1))
                    v.reciprocal(rrec[:, 2 * b:2 * b + 2], rsum[:, 2 * b:2 * b + 2])
                    settle()
                    v.tensor_scalar(probs[:, b, 0:P], probs[:, b, 0:P], rrec[:, 2 * b:2 * b + 1], None, ALU.mult)
                    v.tensor_scalar(probs[:, b, P:384], probs[:, b, P:384], rrec[:, 2 * b + 1:2 * b + 2], None, ALU.mult) \
                        .then_inc(prob_ready, 1)
                dve.wait_ge(ydsa_upd, nth(ydsa_upd, l, 1))
                v.tensor_tensor(ydsa_low[:, :, :].rearrange("p a b -> p (a b)"), wide(6),
                                ydsa_up[:, :, :].bitcast(F32).rearrange("p a b -> p (a b)"), ALU.subtract).then_inc(ydsa_done, 1)
                for nb in range(2):
                    for b in range(3):
                        j = 3 * nb + b
                        dve.wait_ge(unit_used, used(l, U_BR + j + 1))
                        gb = 8 * (0, 2, 1)[b] + 4 * nb
                        gt = gates[:, gb:gb + 4, :].rearrange("p a b -> p (a b)")
                        dst = (mtmp if b else mrg)[:, :, :].rearrange("p a b -> p (a b)")
                        if b == 0 and nb == 1:
                            dve.wait_ge(mrg_up, nth(mrg_up, l, 1))
                        v.scalar_tensor_tensor(out=dst, in0=gt, scalar=1.0, in1=wide(2 * (j % 2)), op0=ALU.add, op1=ALU.mult) \
                            .then_inc(br_used, 1)
                        settle()
                        if b:
                            o = v.tensor_tensor(mrg[:, :, :], mrg[:, :, :], mtmp[:, :, :], ALU.add)
                            if b == 2:
                                o.then_inc(mrg_ready, 1)
                            settle()
                        if j in (0, 3):
                            lower(32 + j)
                    dve.wait_ge(mrg_up, nth(mrg_up, l, nb + 1))
                    v.scalar_tensor_tensor(out=h_low[:, 4 * nb:4 * nb + 4, :], in0=mrg[:, :, :], scalar=0.5,
                                           in1=h_up[:, 4 * nb:4 * nb + 4, :].bitcast(F32), op0=ALU.mult, op1=ALU.subtract) \
                        .then_inc(mrg_done, 1)
                    settle()
                lower(38)
                o_stage(0)
                x_stage(1, Q_FFN)

                taps = prm[:, Q_CB:NPRM].rearrange("p (w g j n) -> p w g j n", w=4, g=2, n=2)

                def conv_params(j):
                    settle()
                    v.tensor_copy(cvp[:, :, :, :], taps[:, :, :, j, :]).then_inc(cvp_ready, 1)

                def conv(half, j, c, base_sig, done):
                    dve.wait_ge(base_sig, nth(base_sig, l, j + 1))
                    for d in (1, 2):
                        for i in range(2):
                            o = v.scalar_tensor_tensor(out=c[:, i, d:T], in0=ps[:, 4 + half, i * T:(i + 1) * T - d],
                                                       scalar=cvp[:, 3 - d, half, i:i + 1], in1=c[:, i, d:T],
                                                       op0=ALU.mult, op1=ALU.add)
                        if d == 1:
                            settle()
                    o.then_inc(done, 1)

                def gated_up(j):
                    settle()
                    dve.wait_ge(gel_done, nth(gel_done, l, j + 1))
                    v.tensor_tensor(gf[:, :, :], gel[:, :, :], cvu[:, :, :], ALU.mult).then_inc(gf_done, 1)

                def g_lower(j, src, dst):
                    dve.wait_ge(gup_done, nth(gup_done, l, j + 1))
                    v.tensor_tensor(dst[:, :, :], gf[:, :, :], src[:, :, :].bitcast(F32), ALU.subtract).then_inc(glow_done, 1)

                conv_params(0)
                lower(41)
                conv(0, 0, cva, cva_base, cva_done)
                conv(1, 0, cvu, cvu_base, cvu_done)
                conv_params(1)
                gated_up(0)
                g_lower(0, g_up, g_low)
                lower(43)
                with dve.Fori(0, NPAIR - 2) as j:
                    lower(44, j)
                    conv(0, j + 1, cva, cva_base, cva_done)
                    conv(1, j + 1, cvu, cvu_base, cvu_done)
                    conv_params(j + 2)
                    gated_up(j + 1)
                    lower(46, j)
                    g_lower(j + 1, g_up, g_low)
                conv(0, NPAIR - 1, cva, cva_base, cva_done)
                conv(1, NPAIR - 1, cvu, cvu_base, cvu_done)
                gated_up(NPAIR - 1)
                g_lower(NPAIR - 1, *g_last)
                o_stage(1)

        @block.gpsimd
        def _(pool):
            pw = nc.gpsimd.tensor_tensor
            for s in low_done:
                pool.sem_inc(s, 1)
            pool.sem_inc(unit_used, SLOTS)
            pool.sem_inc(x_new, 4)
            pool.wait_ge(n_var, 1)
            pw(rs[:, 0:1], ss[:, 0:1], nhalf[:, 0:1], ALU.pow).then_inc(n_rs, 1)
            pool.wait_ge(setup_cp, 1)
            pool.dma_start(scratch.rearrange("t h c -> h t c"), brow[0:HD, None, :].broadcast_to([HD, BIAS_ROWS, 384])).then_inc(bias_out, 16)
            pool.dma_start(kc[:, K_MAT:K_OH], consts[:, K_MAT:K_OH]).then_inc(masks_in, 16)

            with pool.Fori(0, DEPTH) as l:
                def lower(u, step=0):
                    split_low(nc.gpsimd, l, u, step)

                def rsqrt(o, i, n, wait, k, done):
                    pool.wait_ge(wait, nth(wait, l, k))
                    pw(o, i, nhalf[:, 0:n], ALU.pow).then_inc(done, 1)

                def stat(i, o, wait, done, stage, t):
                    rsqrt(o[:, t:t + 1], i[:, t:t + 1], 1, wait, 2 * stage + t + 1, done)

                stat(ss, rs, n_var, n_rs, 0, 1)
                lower_share(l, 1, nc.gpsimd, low_done[0])
                lower(2)
                lower(3)
                rsqrt(cr4, cs4, 4, cvar, 1, crs)
                for u in range(4, 17):
                    if pool_low[u % SLOTS]:
                        lower(u)
                    if u == 6:
                        pool.wait_ge(bias_out, 16)
                        for t in range(0, P, BIAS_ROWS):
                            skew = bass.AP(scratch.tensor, P - t, [[HD * 384 - 1, BIAS_ROWS], [384, HD], [1, T]])
                            pool.dma_start(bias[t:t + BIAS_ROWS, :, :], skew).then_inc(bias_in, 16)
                    if u == 15:
                        rsqrt(bnr2, bnr, 8, bn_var, 1, bn_rs)

                def masked_bias(h):
                    b = h % 2
                    if h == 0:
                        pool.wait_ge(chosen, nth(chosen, l, 1))
                        pool.wait_ge(bias_in, nth(bias_in, l, 16 * P // BIAS_ROWS))
                    if h >= 2:
                        pool.wait_ge(nmax_ready, nth(nmax_ready, l, h - 1))
                    pw(mbias[:, b, 0:P], score[:, 0:P], bias[:, h, P:T], ALU.add)
                    pw(mbias[:, b, P:384], score[:, P:384], bias[:, h, :], ALU.add).then_inc(mb_ready, 1)

                for u in range(17, 40):
                    if pool_low[u % SLOTS] if u < U_FF else pool_low_ffn[u % SLOTS]:
                        lower(u)
                    if u == 19:
                        rsqrt(hrs, hss, 2, ohg_var, 1, ohg_rs)
                        masked_bias(0)
                        masked_bias(1)
                    if 22 <= u < 28:
                        masked_bias(u - 20)
                stat(oss, ors, o_var, o_rs, 0, 0)
                stat(ss, rs, n_var, n_rs, 1, 0)
                stat(oss, ors, o_var, o_rs, 0, 1)
                stat(ss, rs, n_var, n_rs, 1, 1)
                lower(40)
                lower(42)
                with pool.Fori(0, NPAIR - 2) as j:
                    lower(45, j)
                lower(UNITS - 1)
                stat(oss, ors, o_var, o_rs, 1, 0)
                stat(oss, ors, o_var, o_rs, 1, 1)
                stat(ss, rs, n_var, n_rs, 2, 0)


_VECTORS = ["ln_mix_pre", "ln_ffn_pre", "dsa_q_norm", "dsa_kv_norm", "hgrn_norm", "hgrn_lb", "ffn_conv_b", "ffn_conv_w"]
_INS = ["x", "rel_bias", "ln_mix_post", "ln_ffn_post", "w_in", "dsa_w_uq", "dsa_w_uk", "dsa_w_uv",
        "w_br_ret", "w_br_dsa", "w_br_hgrn", "w_out", "ffn_w_up", "ffn_w_down"]


def kernel(**inputs):
    import concourse.bacc as bacc
    from concourse.bass_utils import run_bass_kernel_spmd

    nc = bacc.Bacc("TRN2", target_bir_lowering=False, num_devices=1)
    vectors = np.concatenate([inputs[n].reshape(inputs[n].shape[0], -1, 128) for n in _VECTORS], axis=1).transpose(2, 0, 1)
    arrays = {"shape_constants": shape_constants(), "channel_parameters": np.ascontiguousarray(vectors)}
    arrays.update({f"in_{n}": np.ascontiguousarray(inputs[n]) for n in _INS})
    args = [nc.dram_tensor(n, a.shape, mybir.dt.from_np(a.dtype), kind="ExternalInput").ap() for n, a in arrays.items()]
    y = nc.dram_tensor("y", (1, T, D), F32, kind="ExternalOutput").ap()
    trunk(nc, *args, y)
    return run_bass_kernel_spmd(nc, [arrays], core_ids=[0]).results[0]["y"]
```
